# Optimizing a Trainium2 kernel written in Bass

```python
import math
import jax
import jax.numpy as jnp
from jax import lax
import numpy as np

D_MODEL = 1024
BATCH = 1
SEQ = 1024
DEPTH = 1
DEC_BATCH = 8
DEC_SEQ = 1
PAST_LEN = 8192
PAGE_SIZE = 128

D_POOL = D_MODEL // 2
D_MLSTM = D_MODEL - D_POOL
POOL_WINDOWS = (2, 4, 8, 16)
POOL_GROUPS = len(POOL_WINDOWS)
POOL_GC = D_POOL // POOL_GROUPS
POOL_BUF = max(POOL_WINDOWS) - 1
NH = 4
DH = D_MLSTM // NH
MLSTM_CHUNK = 64
D_FF = 4 * D_MODEL
IN_DIM = D_POOL + 4 * D_MLSTM + 2 * NH
ALPHA = (2.0 * DEPTH) ** 0.25
BETA = (8.0 * DEPTH) ** -0.25
LN_EPS = 1e-5

kernel_name = "hymba_pool_mlstm_deepnorm_step"

def _layer_norm(x, g, b):
    xf = x.astype(jnp.float32)
    mu = jnp.mean(xf, axis=-1, keepdims=True)
    xc = xf - mu
    var = jnp.mean(xc * xc, axis=-1, keepdims=True)
    return (xc * lax.rsqrt(var + LN_EPS) * g.astype(jnp.float32) + b.astype(jnp.float32)).astype(x.dtype)

def _pool_mixer(u, buf, pos0, w_pool, pool_scale):
    bsz, t_len, _ = u.shape
    full_in = jnp.concatenate([buf.astype(u.dtype), u], axis=1)
    full = full_in.astype(jnp.float32)
    cs = jnp.cumsum(full, axis=1)
    cs = jnp.concatenate([jnp.zeros_like(cs[:, :1]), cs], axis=1)
    end = cs[:, POOL_BUF + 1:]
    pos = pos0 + jnp.arange(t_len)
    means = []
    for g, w in enumerate(POOL_WINDOWS):
        lo, hi = g * POOL_GC, (g + 1) * POOL_GC
        s0 = POOL_BUF + 1 - w
        start = cs[:, s0:s0 + t_len, lo:hi]
        cnt = jnp.minimum(pos + 1, w).astype(jnp.float32)[None, :, None]
        means.append((end[..., lo:hi] - start) / cnt)
    pooled = jnp.concatenate(means, axis=-1) - full[:, POOL_BUF:]
    mixed = jnp.einsum('btgc,gcd->btgd', pooled.reshape(bsz, t_len, POOL_GROUPS, POOL_GC),
                       w_pool.astype(jnp.float32)).reshape(bsz, t_len, D_POOL)
    mixed = mixed * pool_scale.astype(jnp.float32)
    new_buf = full_in[:, -POOL_BUF:]
    return mixed, new_buf

def _mlstm(q, k, v, ig, fg, C0, n0, m0):
    bsz, t_len = q.shape[0], q.shape[1]
    L = math.gcd(t_len, MLSTM_CHUNK)
    nc = t_len // L
    f32 = jnp.float32
    qf = q.astype(f32)
    kf = k.astype(f32) * (DH ** -0.5)
    vf = v.astype(f32)
    logf = jax.nn.log_sigmoid(fg.astype(f32))
    igf = ig.astype(f32)

    def chunks(a):
        return a.reshape(bsz, nc, L, NH, DH).transpose(1, 0, 3, 2, 4)

    def gchunks(a):
        return a.reshape(bsz, nc, L, NH).transpose(1, 0, 3, 2)

    causal = jnp.tril(jnp.ones((L, L), dtype=bool))

    def step(carry, xs):
        C, n, m = carry
        qc, kc, vc, ic, lfc = xs
        b = jnp.cumsum(lfc, axis=-1)
        D = b[..., :, None] - b[..., None, :] + ic[..., None, :]
        D = jnp.where(causal, D, -jnp.inf)
        inter = b + m[..., None]
        m_t = jnp.maximum(inter, jnp.max(D, axis=-1))
        Dw = jnp.exp(D - m_t[..., None])
        iw = jnp.exp(inter - m_t)
        s = jnp.einsum('bhtd,bhsd->bhts', qc, kc) * Dw
        num = jnp.einsum('bhts,bhse->bhte', s, vc) + iw[..., None] * jnp.einsum('bhtd,bhde->bhte', qc, C)
        den = jnp.sum(s, axis=-1) + iw * jnp.einsum('bhtd,bhd->bht', qc, n)
        h = num / jnp.maximum(jnp.abs(den), jnp.exp(-m_t))[..., None]
        m_new = m_t[..., -1]
        g_state = jnp.exp(b[..., -1] + m - m_new)
        w_s = jnp.exp(b[..., -1:] - b + ic - m_new[..., None])
        C_new = g_state[..., None, None] * C + jnp.einsum('bhs,bhsd,bhse->bhde', w_s, kc, vc)
        n_new = g_state[..., None] * n + jnp.einsum('bhs,bhsd->bhd', w_s, kc)
        return (C_new, n_new, m_new), h

    carry0 = (C0.astype(f32), n0.astype(f32), m0.astype(f32))
    (C1, n1, m1), hs = lax.scan(step, carry0, (chunks(qf), chunks(kf), chunks(vf), gchunks(igf), gchunks(logf)))
    h = hs.transpose(1, 0, 3, 2, 4).reshape(bsz, t_len, NH * DH)
    return h, C1, n1, m1

def _layer(x, pool_buf, C, n, m, pos0, w_in, b_gate, w_pool, pool_scale, w_out,
           ln1_g, ln1_b, w_ff1, b_ff1, w_ff2, b_ff2, ln2_g, ln2_b):
    bsz, t_len, _ = x.shape
    proj = x @ w_in
    cuts = [D_POOL, D_POOL + D_MLSTM, D_POOL + 2 * D_MLSTM, D_POOL + 3 * D_MLSTM, D_POOL + 4 * D_MLSTM]
    u_pool, q, k, v, o_pre, gates = jnp.split(proj, cuts, axis=-1)
    gates = gates.astype(jnp.float32) + b_gate.astype(jnp.float32)
    ig, fg = gates[..., :NH], gates[..., NH:]
    y_pool, new_buf = _pool_mixer(u_pool, pool_buf, pos0, w_pool, pool_scale)
    hd = (bsz, t_len, NH, DH)
    h, C1, n1, m1 = _mlstm(q.reshape(hd), k.reshape(hd), v.reshape(hd), ig, fg, C, n, m)
    y_ml = jax.nn.sigmoid(o_pre.astype(jnp.float32)) * h
    mix = jnp.concatenate([y_pool, y_ml], axis=-1).astype(x.dtype) @ w_out
    x1 = _layer_norm(ALPHA * x + mix, ln1_g, ln1_b)
    ff = jnp.square(jax.nn.relu(x1 @ w_ff1 + b_ff1)) @ w_ff2 + b_ff2
    x2 = _layer_norm(ALPHA * x1 + ff, ln2_g, ln2_b)
    dt = x.dtype
    return x2, new_buf.astype(dt), C1.astype(dt), n1.astype(dt), m1.astype(dt)

def setup_inputs(seed: int = 0) -> dict:
    key = jax.random.key(seed)
    ks = jax.random.split(key, 24)
    nrm = jax.random.normal
    f32 = jnp.float32
    x_prompt = nrm(ks[0], (BATCH, SEQ, D_MODEL), f32)
    x_sample = nrm(ks[1], (DEC_BATCH, DEC_SEQ, D_MODEL), f32)
    state_pool = nrm(ks[2], (DEPTH, DEC_BATCH, POOL_BUF, D_POOL), f32)
    state_C = 0.5 * nrm(ks[3], (DEPTH, DEC_BATCH, NH, DH, DH), f32)
    state_n = 0.5 * nrm(ks[4], (DEPTH, DEC_BATCH, NH, DH), f32)
    state_m = nrm(ks[5], (DEPTH, DEC_BATCH, NH), f32)
    w_in = nrm(ks[6], (DEPTH, D_MODEL, IN_DIM), f32) * D_MODEL ** -0.5
    i_bias = 0.1 * nrm(ks[7], (DEPTH, NH), f32)
    f_bias = jnp.broadcast_to(jnp.linspace(3.0, 6.0, NH, dtype=f32), (DEPTH, NH)) + 0.1 * nrm(ks[8], (DEPTH, NH), f32)
    b_gate = jnp.concatenate([i_bias, f_bias], axis=-1)
    w_pool = nrm(ks[9], (DEPTH, POOL_GROUPS, POOL_GC, POOL_GC), f32) * POOL_GC ** -0.5
    pool_scale = 1.0 + 0.02 * nrm(ks[10], (DEPTH, D_POOL), f32)
    w_out = nrm(ks[11], (DEPTH, D_MODEL, D_MODEL), f32) * (D_MODEL ** -0.5) * BETA
    ln1_g = 1.0 + 0.02 * nrm(ks[12], (DEPTH, D_MODEL), f32)
    ln1_b = 0.02 * nrm(ks[13], (DEPTH, D_MODEL), f32)
    w_ff1 = nrm(ks[14], (DEPTH, D_MODEL, D_FF), f32) * D_MODEL ** -0.5
    b_ff1 = 0.02 * nrm(ks[15], (DEPTH, D_FF), f32)
    w_ff2 = nrm(ks[16], (DEPTH, D_FF, D_MODEL), f32) * (D_FF ** -0.5) * BETA
    b_ff2 = 0.02 * nrm(ks[17], (DEPTH, D_MODEL), f32)
    ln2_g = 1.0 + 0.02 * nrm(ks[18], (DEPTH, D_MODEL), f32)
    ln2_b = 0.02 * nrm(ks[19], (DEPTH, D_MODEL), f32)
    return {"x_prompt": x_prompt, "x_sample": x_sample,
            "state_pool": state_pool, "state_C": state_C, "state_n": state_n, "state_m": state_m,
            "w_in": w_in, "b_gate": b_gate, "w_pool": w_pool, "pool_scale": pool_scale,
            "w_out": w_out, "ln1_g": ln1_g, "ln1_b": ln1_b, "w_ff1": w_ff1, "b_ff1": b_ff1,
            "w_ff2": w_ff2, "b_ff2": b_ff2, "ln2_g": ln2_g, "ln2_b": ln2_b}

def reference(x_prompt, x_sample, state_pool, state_C, state_n, state_m,
              w_in, b_gate, w_pool, pool_scale, w_out, ln1_g, ln1_b,
              w_ff1, b_ff1, w_ff2, b_ff2, ln2_g, ln2_b):
    f32 = jnp.float32
    bp = x_prompt.shape[0]
    yp, ys = x_prompt, x_sample
    pp, Cp, np_, mp = [], [], [], []
    ps, Cs, ns, ms = [], [], [], []
    for l in range(DEPTH):
        wts = (w_in[l], b_gate[l], w_pool[l], pool_scale[l], w_out[l], ln1_g[l], ln1_b[l],
               w_ff1[l], b_ff1[l], w_ff2[l], b_ff2[l], ln2_g[l], ln2_b[l])
        buf0 = jnp.zeros((bp, POOL_BUF, D_POOL), yp.dtype)
        C0 = jnp.zeros((bp, NH, DH, DH), f32)
        n0 = jnp.zeros((bp, NH, DH), f32)
        m0 = jnp.zeros((bp, NH), f32)
        yp, b1, c1, n1, m1 = _layer(yp, buf0, C0, n0, m0, 0, *wts)
        pp.append(b1); Cp.append(c1); np_.append(n1); mp.append(m1)
        ys, b2, c2, n2, m2 = _layer(ys, state_pool[l], state_C[l], state_n[l], state_m[l], PAST_LEN, *wts)
        ps.append(b2); Cs.append(c2); ns.append(n2); ms.append(m2)
    return (yp, ys,
            jnp.stack(pp), jnp.stack(Cp), jnp.stack(np_), jnp.stack(mp),
            jnp.stack(ps), jnp.stack(Cs), jnp.stack(ns), jnp.stack(ms))


_drawn_inputs = setup_inputs


def setup_inputs(seed=0):
    import zlib

    import numpy as np

    out = dict(_drawn_inputs(seed))
    spreads = {}
    factors = {'pool_scale': 21.752,
     'ln1_g': 2.777,
     'b_ff1': 4.704,
     'b_ff2': 18.593,
     'ln2_g': 8.333,
     'ln2_b': 8.223,
     'ln1_b': 6.832}
    for name, (base, spread) in spreads.items():
        noise = np.random.default_rng([zlib.crc32(name.encode()), seed]).standard_normal(out[name].shape)
        drawn = base * np.exp(spread * noise) if base else spread * noise
        out[name] = jnp.asarray(drawn.astype(out[name].dtype))
    for name, factor in factors.items():
        out[name] = (out[name] * factor).astype(out[name].dtype)
    return out
```

```python
from contextlib import ExitStack

import concourse.bass as bass
from concourse import mybir

F32, F32R = mybir.dt.float32, mybir.dt.float32r
ACT = mybir.ActivationFunctionType
ALU = mybir.AluOpType
AX = mybir.AxisListType

P = 128
SEQ, NS = 1024, 8
D = 1024
KC = D // P
NT = SEQ + NS
NBLK = 3
BLK = NT // NBLK
NH, DH = 4, 128
WINDOWS = (2, 4, 8, 16)
NBUF = max(WINDOWS) - 1
NCH = SEQ // P
DFF = 4 * D
FG = 512
NG = DFF // FG
UW = 256
ALPHA = 2.0 ** 0.25
EPS = 1e-5
TILES = [(BLK * b + P * j, min(P, BLK - P * j)) for b in range(NBLK) for j in range(3)]
PROJ = [("A", 0), ("B", 0), ("A", 1), ("B", 1), ("A", 2), ("B", 2), ("A", 3), ("B", 3), ("U", 1), ("U", 0)]
U_OUT = 1 + len(PROJ)
U_FFN = U_OUT + NBLK * (D // UW)
N_GATE = NBLK
N_PROJ = N_GATE + 6 * len(PROJ)
N_OUT = N_PROJ + NBLK * KC
GATE_ROWS = 36
PAIRS = NCH // 2


def build_layer(nc, a):
    ctx = ExitStack()
    with ctx:
        base = (nc.sbuf_base + 63) // 64 * 64
        R = {}

        def at(name, shape, off, dt=F32):
            size = 4
            for s in shape[1:]:
                size *= s
            R[name] = off + size
            return nc.alloc_sbuf_tensor_at(name, shape, dt, offset=base + off)

        XROW = NT * 4
        o_xh, o_xl, o_r1 = 0, KC * XROW, 2 * KC * XROW
        o_r2 = 3 * KC * XROW
        o_raw = 4 * KC * XROW
        o_wh = o_raw + 2 * KC * UW * 4
        o_wl = o_wh + 2 * KC * UW * 4
        o_att = o_wl + 2 * KC * UW * 4
        XH = at("x_hi", [P, KC, NT], o_xh, F32R)
        XL = at("x_lo", [P, KC, NT], o_xl, F32R)
        Y = at("y_acc", [P, KC, NT], o_r1)
        RAW = at("w_raw", [P, 2, KC * UW], o_raw)
        WH = at("w_hi", [P, 2, KC * UW], o_wh, F32R)
        WL = at("w_lo", [P, 2, KC * UW], o_wl, F32R)
        QKV = [at("qkv0", [P, 3, NT], o_r2 + 3 * XROW), at("qkv1", [P, 3, NT], o_r2)]
        C0 = at("sample_C", [P, NH, NS, DH], o_r2 + 3 * XROW)
        TB = at("win_b", [P, 8 + NT], o_r2 + 3 * XROW + 16384)
        HH = at("h_hi", [P, FG // P, NT], o_r2, F32R)
        HL = at("h_lo", [P, FG // P, NT], o_r2 + 4 * XROW, F32R)
        XNAT = at("x_nat_all", [P, len(TILES), D], o_r1)
        SPN = at("state_pool_nat", [P, 4 * P], o_r2 + 3 * XROW + 16384)
        CN = at("const_nat", [P, P], o_r2 + 3 * XROW + 16384 + 2048)
        SPT = at("state_pool_T", [P, 4, NS, NBUF], o_r2 + 4096)
        row = lambda name, ch: at(name, [P, NT], o_r1 + ch * XROW)
        RC = row("gate_rows", 0)
        TI, TF, TBS = row("row_i", 1), row("row_f", 2), row("row_b", 3)
        TM, TN, TZ = row("row_m", 5), row("row_negM", 6), row("row_z", 7)
        cur = [o_att]

        def put(name, shape, dt=F32):
            t = at(name, shape, cur[0], dt)
            cur[0] = (R[name] + 31) // 32 * 32
            return t

        IDN = put("identity", [P, P])
        ONES = put("ones", [P, P])
        CST = put("const_T", [P, 92])
        BC = put("bc_cols", [P, 4, NH, NS])
        COLS = put("gate_cols", [P, NCH, 4, NH])
        SM = put("sample_qkv", [P, 3, NH, NS])
        ST = put("sample_tmp", [P, 10, NH, NS])
        US = put("u_last", [P, 4, NBUF + NS])
        NO = put("n_out", [P, 36])
        WSUM = put("win_state", [P, 4, NS])
        SMALL = put("small", [P, 64])
        INV = put("inv_count", [P, 16])
        TAIL = SMALL[:, 49:64]
        LNT = put("ln_stats", [P, 2, 20])
        o_lay = cur[0]
        E = put("decay", [P, 2, P])
        PT = put("probs", [P, 2, P])
        KW = put("k_weighted", [P, 2, P])
        QI = put("q_inter", [P, 2, P])
        HN = put("h_nat", [P, 2, P])
        VA = put("v_aug", [P, 2, DH + 1])
        CA = put("state_ring", [P, 3, DH + 1])
        WP = put("w_pool_sb", [P, 4, P])
        RBH = put("rows_hi", [P, NT], F32R)
        o_xn = R["rows_hi"] - XROW
        RBL = put("rows_lo", [P, NT], F32R)
        SEL = put("select", [P, 2, NH, P], F32R)
        TA = put("win_a", [P, 8 + NT])
        assert base + cur[0] <= nc.sbuf_usable_end, (base + cur[0], nc.sbuf_usable_end)
        VM = at("v_masked", [P, 2, 4, P], o_lay)
        KVN = at("kv_sample_nat", [P, 2, P], o_lay + 4096)
        XV = at("x1_T", [P, KC, P], o_lay)
        RT = at("relu", [P, 2, BLK], o_lay + 4096)
        SQ = at("relu_sq", [P, 2, BLK], o_lay + 4096 + 2 * BLK * 4)
        assert R["relu_sq"] <= o_xn
        XN = at("x_nat", [P, 2, D], o_xn)
        RS = at("res_nat", [P, 2, D], o_xn + 8192)
        GB = at("ln2_gb", [P, 2, D], o_xn)
        OUT = [at("out0", [P, D], o_xn + 8192), at("out1", [P, D], o_xn + 12288), at("out2", [P, D], o_lay)]
        UN = at("u_nat", [P, 4 * P], o_xn)
        NN = at("n_nat", [P, P], o_xn + 2048)

        bank = [ctx.enter_context(nc.psum_tensor(f"bank{i}", [P, 512], F32)) for i in range(8)]
        B_, S_, T_, D_, N_ = bank[3:8]

        def sem(name):
            return ctx.enter_context(nc.semaphore(name))

        raw_in = [sem("raw_in0"), sem("raw_in1")]
        hi_done, lo_done = sem("hi_done"), sem("lo_done")
        gemm_done, gemm_read = sem("gemm_done"), sem("gemm_read")
        x_in = [sem(f"x_in{b}") for b in range(NBLK)]
        small_in, bias_in, consts = sem("small_in"), sem("bias_in"), sem("consts")
        xT_ready, x_hi, x_lo = sem("xT_ready"), sem("x_hi_done"), sem("x_lo_done")
        stT_ready, stT_read = sem("stT_ready"), sem("stT_read")
        act_row, dve_row = sem("act_row"), sem("dve_row")
        colT, colT_read = sem("colT"), sem("colT_read")
        pool_step, smp_kept, wsum_ready = sem("pool_step"), sem("smp_kept"), sem("wsum_ready")
        bc_ready, s_ready, kvT_ready = sem("bc_ready"), sem("s_ready"), sem("kvT_ready")
        dC_ready, num_ready = sem("dC_ready"), sem("num_ready")
        E_ready, Em_ready, v_ready = sem("E_ready"), sem("Em_ready"), sem("v_ready")
        hn_ready, P_ready, kw_ready, qi_ready = sem("hn_ready"), sem("P_ready"), sem("kw_ready"), sem("qi_ready")
        C_ready, den_ready, r_ready, y_ready = sem("C_ready"), sem("den_ready"), sem("r_ready"), sem("y_ready")
        ncol_ready, state_out = sem("ncol_ready"), sem("state_out")
        c_in, prod_ready, smp_num = sem("c_in"), sem("prod_ready"), sem("smp_num")
        smp, smp_y, smp_n = sem("smp_step"), sem("smp_y"), sem("smp_n")
        kvs_T, kvs_read, vm_ready, outer_ready = sem("kvs_T"), sem("kvs_read"), sem("vm_ready"), sem("outer_ready")
        C_new, c_out = sem("C_new"), sem("c_out")
        win_step, pooled, mixed, mixed_read = sem("win_step"), sem("pooled"), sem("mixed"), sem("mixed_read")
        nat_T, nat_read, nat_out, outs = sem("nat_T"), sem("nat_read"), sem("nat_out"), sem("outs")
        cat_hi, cat_lo = sem("cat_hi"), sem("cat_lo")
        xn_in = [sem("xn_in0"), sem("xn_in1")]
        mixT_ready, res_done, ln_dve, ln_sqrt, ln_norm = (
            sem("mixT_ready"), sem("res_done"), sem("ln_dve"), sem("ln_sqrt"), sem("ln_norm"))
        nT_ready, xv_ready, x1_hi, x1_lo, x1_acc = (
            sem("nT_ready"), sem("xv_ready"), sem("x1_hi"), sem("x1_lo"), sem("x1_acc"))
        bf_ready, sq_done, h_hi, h_lo = sem("bf_ready"), sem("sq_done"), sem("h_hi"), sem("h_lo")
        down_done, down_read = sem("down_done"), sem("down_read")
        ln_aggr, l2_aggr = sem("ln_aggr"), sem("l2_aggr")
        gb_in, l2_T, l2_dve, l2_sqrt, l2_norm, l2_g, l2_b = (
            sem("gb_in"), sem("l2_T"), sem("l2_dve"), sem("l2_sqrt"), sem("l2_norm"), sem("l2_g"), sem("l2_b"))
        out_done = [sem(f"out_done{i}") for i in range(3)]

        block = ctx.enter_context(nc.Block())

        def wslot(t, s):
            return t[:, s % 2, :].rearrange("p (k n) -> p k n", k=KC)

        def wslot2(t, s):
            return t[:, s % 2, :].rearrange("p (k n) -> p k n", k=FG // P)

        def gslot(t):
            return t[:, 0, 0:KC * GATE_ROWS].rearrange("p (k n) -> p k n", k=KC)

        def blk(b):
            return slice(BLK * b, BLK * (b + 1))

        w_in_v = a["w_in"][0].rearrange("(k p) n -> p k n", p=P)
        w_out_v = a["w_out"][0].rearrange("(k p) n -> p k n", p=P)
        w1_v = a["w_ff1"][0].rearrange("(k p) n -> p k n", p=P)
        w2_v = a["w_ff2"][0].rearrange("(k p) n -> p k n", p=P)
        G1, B1, B2, PS, BF = 0, 8, 16, 24, 28
        n0T = CST[:, 60:92].rearrange("p (b h) -> p h b", h=NH)
        pr, sa = slice(0, SEQ), slice(SEQ, NT)

        raw_count = [0, 0]
        RAW_AT = []
        for u in range(U_FFN):
            raw_count[u % 2] += 32 if 1 <= u <= 8 else 16
            RAW_AT.append(raw_count[u % 2])

        def outputs_to(u):
            return N_GATE + 6 * u if u < U_OUT else N_PROJ + 2 * (u - U_OUT + 1)

        def ffn_raw(i):
            return raw_count[(U_FFN + i) % 2] + 16 * (i // 2 + 1)

        def token_dma(eng, tile, dram_p, dram_s, t, to_sbuf, s):
            t0, n = TILES[t]
            np_ = min(n, SEQ - t0)
            parts = [(tile[0:np_, :], dram_p[0, t0:t0 + np_, :])]
            if np_ < n:
                parts.append((tile[np_:n, :], dram_s[:, 0, :]))
            for sb, dr in parts:
                if to_sbuf:
                    eng.dma_start(sb, dr).then_inc(s, 16)
                else:
                    eng.dma_start(dr, sb).then_inc(s, 16)

        def arrived(t, n_slots):
            return 16 * (t // n_slots + 1 + (t == len(TILES) - 1))

        def pair(p):
            h, j = p // PAIRS, p % PAIRS
            return h, j, slice(2 * P * j, 2 * P * (j + 1))

        def gap_pair(u, i):
            gap = 6 * (u - 3) + i
            return (gap % 3, gap // 3) if gap >= 0 else (None, None)

        UCH = {(9, 0): 3, (9, 1): 2, (10, 0): 1, (10, 1): 0}
        ROW_PAD, ROW_INV, ROW_M, ROW_NEGM, ROW_Z, ROW_A, ROW_W, ROW_LO, ROW_RX = 1, 2, 6, 7, 8, 9, 10, 11, 12
        NPAIR = NH * PAIRS

        @block.sync
        def _(sp):
            for t in range(3):
                token_dma(sp, XNAT[0:TILES[t][1], t, :], a["x_prompt"], a["x_sample"], t, True, x_in[0])
            with nc.allow_non_contiguous_dma(reason="eight gate columns"):
                sp.dma_start(wslot(RAW, 0)[:, :, 0:2 * NH], w_in_v[:, :, 2560:2568]).then_inc(raw_in[0], 16)
            for t in range(3, len(TILES)):
                token_dma(sp, XNAT[0:TILES[t][1], t, :], a["x_prompt"], a["x_sample"], t, True, x_in[t // 3])
            for u in range(1, U_OUT):
                kind, j = PROJ[u - 1]
                if u >= 2:
                    sp.wait_ge(lo_done, u - 1)
                slot = wslot(RAW, u)
                if kind == "U":
                    sp.dma_start(slot, w_in_v[:, :, UW * j:UW * (j + 1)]).then_inc(raw_in[u % 2], 16)
                else:
                    for s in range(2):
                        c = 512 + 512 * s + DH * j + (1024 if kind == "B" else 0)
                        sp.dma_start(slot[:, :, P * s:P * (s + 1)], w_in_v[:, :, c:c + P]).then_inc(raw_in[u % 2], 16)
            for u in range(U_OUT, U_FFN):
                j = (u - U_OUT) % (D // UW)
                sp.wait_ge(lo_done, u - 1)
                sp.dma_start(wslot(RAW, u), w_out_v[:, :, UW * j:UW * (j + 1)]).then_inc(raw_in[u % 2], 16)
            with sp.Fori(0, NG) as g:
                for i in range(4):
                    s = U_FFN + i
                    sp.wait_ge(lo_done, g * 4 + (s - 1))
                    if i < 2:
                        src, dst = w1_v[:, :, bass.ds(g * FG + UW * i, UW)], wslot(RAW, s)
                    else:
                        src = w2_v[:, bass.ds(g * (FG // P), FG // P), 512 * (i - 2):512 * (i - 1)]
                        dst = wslot2(RAW, s)
                    sp.dma_start(dst, src).then_inc(raw_in[s % 2], 16)
            for t in range(len(TILES)):
                sp.wait_ge(l2_b, t + 1)
                token_dma(sp, OUT[t % 3][0:TILES[t][1], :], a["y_prompt"], a["y_sample"], t, False, out_done[t % 3])
            for s in range(3):
                sp.wait_ge(out_done[s], arrived(6 + s, 3))

        def x1_hi_part(pool, t):
            t0, n = TILES[t]
            pool.wait_ge(xv_ready, KC * (t + 1))
            nc.gpsimd.tensor_copy(XH[:, :, t0:t0 + n], XV[:, :, 0:n]).then_inc(x1_hi, 1)

        def norm1(pool, t):
            t0, n = TILES[t]
            q = t % 2
            pool.wait_ge(ln_dve, 4 * t + 4)
            nc.gpsimd.tensor_scalar(RS[0:n, q, :], RS[0:n, q, :], LNT[0:n, q, 16:17], LNT[0:n, q, 17:18],
                                    ALU.mult, ALU.add).then_inc(ln_norm, 1)

        @block.gpsimd
        def _(pool):
            G = nc.gpsimd
            G.memset(IDN[:, :], 0.0).then_inc(pool_step, 1)
            pool.wait_ge(pool_step, 1)
            G.affine_select(out=IDN[:, :], in_=IDN[:, :], compare_op=ALU.not_equal, fill=1.0, base=0,
                            pattern=[[-1, P]], channel_multiplier=1).then_inc(consts, 1)
            G.memset(ONES[:, :], 1.0).then_inc(consts, 1)
            sel = TA[:, 0:2 * NH * P].rearrange("p (g h m) -> p g h m", g=2, h=NH)
            G.memset(sel, 0.0).then_inc(pool_step, 1)
            pool.wait_ge(pool_step, 2)
            G.affine_select(out=sel, in_=sel, compare_op=ALU.not_equal, fill=1.0, base=0,
                            pattern=[[-32, 2], [-1, NH], [0, P]], channel_multiplier=1).then_inc(pool_step, 1)
            pool.wait_ge(pool_step, 3)
            G.tensor_copy(SEL[:, :, :, :], sel).then_inc(consts, 1)
            G.memset(VA[:, :, DH:DH + 1], 1.0).then_inc(consts, 1)
            pool.wait_ge(xT_ready, 2 * len(TILES))
            G.memset(RC[:, :], 0.0).then_inc(consts, 1)
            G.memset(TN[0:NH, :], 1.0).then_inc(pool_step, 1)
            pool.wait_ge(pool_step, 4)
            G.memset(TN[0:NH, pr].rearrange("h (c t) -> h c t", t=P)[:, :, 0:1], 0.0).then_inc(consts, 1)
            pool.dma_start(a["pool_s"][0, :, 0:NBUF - 1, :], a["state_pool"][0, :, 1:NBUF, :]).then_inc(outs, 16)

            def keep(h, js):
                for j in js:
                    pool.wait_ge(gemm_read, N_GATE + 12 * h + 3 * j + 3)
                    G.tensor_copy(SM[:, j, h, :], QKV[h % 2][:, j, sa]).then_inc(smp_kept, 1)

            def mask(p):
                pool.wait_ge(E_ready, 2 * (p + 1))
                G.affine_select(out=E[:, :, :], in_=E[:, :, :], compare_op=ALU.is_ge, fill=0.0, base=0,
                                pattern=[[0, 2], [1, P]], channel_multiplier=-1).then_inc(Em_ready, 1)

            def final_state(h):
                pool.wait_ge(C_ready, NCH * (h + 1))
                pool.dma_start(a["C_p"][0, 0, h, :, :], CA[:, NCH % 3, 0:DH]).then_inc(state_out, 16)

            keep(0, (0, 1, 2))
            pool.wait_ge(dve_row, ROW_Z)
            with nc.allow_non_contiguous_dma(reason="a few words"):
                pool.dma_start(a["m_p"][0, 0:1, :].rearrange("a h -> h a"), SMALL[0:NH, 40:41]).then_inc(outs, 16)
                pool.dma_start(a["m_s"][0].rearrange("b h -> h b"), SMALL[0:NH, 41:49]).then_inc(outs, 16)
            for h in range(NH):
                for j in range(PAIRS):
                    mask(PAIRS * h + j)
                    if h < NH - 1 and j == 2:
                        keep(h + 1, (0, 1))
                if h < NH - 1:
                    keep(h + 1, (2,))
                final_state(h)
                if h == NH - 2:
                    pool.wait_ge(num_ready, PAIRS * (NH - 1))
                    for s in range(NH):
                        pool.dma_start(C0[:, s, :, :], a["state_C"][0, :, s, :, :].rearrange("b d e -> d b e"))\
                            .then_inc(c_in, 16)
            pool.wait_ge(nat_read, 1)
            pool.dma_start(a["pool_p"][0, 0, :, :], UN[0:NBUF, :]).then_inc(nat_out, 16)
            pool.dma_start(a["pool_s"][0, :, NBUF - 1, :], UN[NBUF:NBUF + NS, :]).then_inc(nat_out, 16)
            pool.wait_ge(nat_read, 2)
            for h in range(NH):
                pool.dma_start(a["n_s"][0, :, h, :], NN[NS * h:NS * (h + 1), :]).then_inc(nat_out, 16)
            pool.dma_start(a["n_p"][0, 0, :, :], NN[32:36, :]).then_inc(nat_out, 16)
            for h in range(NH):
                pool.wait_ge(C_new, NS * (h + 1))
                pool.dma_start(a["C_s"][0, :, h, :, :].rearrange("b d e -> d b e"), C0[:, h, :, :]).then_inc(c_out, 16)
            pool.wait_ge(nat_out, 16 * 7)
            for t in range(len(TILES)):
                for x in ((0, 1) if t == 0 else (t + 1,)):
                    if x < len(TILES):
                        if x >= 2:
                            pool.wait_ge(res_done, x - 1)
                        token_dma(pool, XN[0:TILES[x][1], x % 2, :], a["x_prompt"], a["x_sample"], x, True, xn_in[x % 2])
                norm1(pool, t)
                if t % 3:
                    x1_hi_part(pool, t - 1)
                if t % 3 == 2:
                    x1_hi_part(pool, t)
            pool.wait_ge(res_done, len(TILES))
            for i, name in enumerate(("ln2_g", "ln2_b")):
                pool.dma_start(GB[:, i, :], a[name][0:1, :].to_broadcast([P, D])).then_inc(gb_in, 16)
            pool.wait_ge(gb_in, 32)
            for t, (t0, n) in enumerate(TILES):
                pool.wait_ge(l2_g, t + 1)
                G.tensor_tensor(OUT[t % 3][0:n, :], OUT[t % 3][0:n, :], GB[0:n, 1, :], ALU.add).then_inc(l2_b, 1)
            pool.wait_ge(outs, 16 * 3)
            pool.wait_ge(c_out, 16 * NH)
            pool.wait_ge(state_out, 16 * NH)

        @block.scalar
        def _(act):
            A = nc.scalar.activation
            r = 0
            for name, n in (("ln1_g", 8), ("ln1_b", 8), ("b_ff2", 8), ("pool_scale", 4), ("b_ff1", 32)):
                act.dma_start(CN[r:r + n, :], a[name][0].rearrange("(n p) -> n p", p=P)).then_inc(small_in, 16)
                r += n
            act.dma_start(CN[r:r + 32, :], a["state_n"][0].rearrange("b h d -> (b h) d")).then_inc(small_in, 16)
            act.dma_start(SPN[0:NS * NBUF, :], a["state_pool"][0].rearrange("b r c -> (b r) c")).then_inc(small_in, 16)
            act.dma_start(WP[:, :, :], a["w_pool"][0].rearrange("g c d -> c g d")).then_inc(small_in, 16)
            with nc.allow_non_contiguous_dma(reason="a few words"):
                act.dma_start(SMALL[0:NH, 0:1], a["b_gate"][0:1, 0:NH].rearrange("a h -> h a")).then_inc(bias_in, 16)
                act.dma_start(SMALL[0:NH, 1:2], a["b_gate"][0:1, NH:2 * NH].rearrange("a h -> h a")).then_inc(bias_in, 16)
                act.dma_start(SMALL[0:NH, 8:16], a["state_m"][0].rearrange("b h -> h b")).then_inc(bias_in, 16)

            def split_hi(u):
                act.wait_ge(raw_in[u % 2], RAW_AT[u])
                if u >= 2:
                    act.wait_ge(gemm_done, outputs_to(u - 2))
                if u == 0:
                    act.wait_ge(dve_row, ROW_PAD)
                    A(gslot(WH)[:, :, 0:NH], wslot(RAW, 0)[:, :, 0:NH], ACT.Copy)
                    A(gslot(WH)[:, :, 32:32 + NH], wslot(RAW, 0)[:, :, NH:2 * NH], ACT.Copy).then_inc(hi_done, 1)
                else:
                    A(WH[:, u % 2, :], RAW[:, u % 2, :], ACT.Copy).then_inc(hi_done, 1)

            for s in range(2 * len(TILES)):
                t0, n = TILES[s // 2]
                act.wait_ge(xT_ready, s + 1)
                A(XH[:, 4 * (s % 2):4 * (s % 2) + 4, t0:t0 + n],
                  bank[3 + s % 4][:, :].rearrange("p (k n) -> p k n", k=4)[:, :, 0:n], ACT.Copy).then_inc(x_hi, 1)
                if s == 5:
                    split_hi(0)
                elif s == 11:
                    split_hi(1)
            act.wait_ge(stT_ready, 1)
            A(CST[:, :], B_[:, 0:92], ACT.Copy).then_inc(stT_read, 1)
            act.wait_ge(stT_ready, 2)
            A(SPT[:, :, :, :].rearrange("p g b r -> p g (b r)"),
              S_[:, :].rearrange("p (g n) -> p g n", g=4)[:, :, 0:NS * NBUF], ACT.Copy).then_inc(stT_read, 1)

            act.wait_ge(bias_in, 16 * 3)
            for b in range(NBLK):
                act.wait_ge(gemm_done, b + 1)
                A(TI[0:NH, blk(b)], bank[b][0:NH, 0:BLK], ACT.Identity, bias=SMALL[0:NH, 0:1])
                A(TF[0:NH, blk(b)], bank[b][32:32 + NH, 0:BLK], ACT.Identity, bias=SMALL[0:NH, 1:2]).then_inc(gemm_read, 1)
            act.wait_ge(gemm_read, NBLK)
            A(TZ[0:NH, :], TF[0:NH, :], ACT.Abs).then_inc(act_row, 1)
            act.wait_ge(act_row, 1)
            A(TM[0:NH, :], TZ[0:NH, :], ACT.Exp, scale=-1.0).then_inc(act_row, 1)
            act.wait_ge(act_row, 2)
            A(TZ[0:NH, :], TM[0:NH, :], ACT.Ln, bias=1.0).then_inc(act_row, 1)
            act.wait_ge(dve_row, ROW_NEGM)
            A(RBH[0:NH, pr], TN[0:NH, pr], ACT.Copy).then_inc(act_row, 1)
            act.wait_ge(dve_row, ROW_Z)
            act.wait_ge(consts, 5)
            A(RC[32:32 + NH, :], TZ[0:NH, :], ACT.Exp).then_inc(act_row, 1)
            A(RC[96:96 + NH, :], TM[0:NH, :], ACT.Exp, scale=-1.0).then_inc(act_row, 1)
            act.wait_ge(dve_row, ROW_W)
            A(RC[64:64 + NH, :], TBS[0:NH, :], ACT.Exp).then_inc(act_row, 1)
            act.wait_ge(act_row, 5)
            A(RBH[32:32 + NH, :], RC[32:32 + NH, :], ACT.Copy).then_inc(act_row, 1)

            def evac(u, i):
                kind, j = PROJ[u - 1]
                f, b = i // 3, i % 3
                n = N_GATE + 6 * (u - 1) + i
                act.wait_ge(gemm_done, n + 1)
                src = bank[n % 3][:, 0:BLK]
                if kind == "U":
                    A(Y[:, UCH[u, f], blk(b)], src, ACT.Copy).then_inc(gemm_read, 1)
                elif kind == "A":
                    if j >= 2 and i == 0:
                        act.wait_ge(smp_kept, 3 * (j - 1))
                    A(QKV[j % 2][:, f, blk(b)], src, ACT.Copy, scale=(DH ** -0.5 if f else 1.0)).then_inc(gemm_read, 1)
                elif f == 0:
                    A(QKV[j % 2][:, 2, blk(b)], src, ACT.Copy).then_inc(gemm_read, 1)
                else:
                    A(Y[:, 4 + j, blk(b)], src, ACT.Sigmoid).then_inc(gemm_read, 1)

            def decay_and_v(p):
                h, j, _ = pair(p)
                act.wait_ge(bc_ready, p + 1)
                if p:
                    act.wait_ge(P_ready, p)
                for i in range(2):
                    A(E[:, i, :], B_[:, P * i:P * (i + 1)], ACT.Exp,
                      bias=COLS[:, 2 * j + i, 0, h:h + 1]).then_inc(E_ready, 1)
                act.wait_ge(kvT_ready, p + 1)
                if p:
                    act.wait_ge(num_ready, p)
                A(VA[:, :, 0:DH], T_[:, 256:512].rearrange("p (i n) -> p i n", i=2), ACT.Copy).then_inc(v_ready, 1)

            def divide(p):
                act.wait_ge(r_ready, p + 1)
                if p:
                    act.wait_ge(s_ready, p + 1)
                for i in range(2):
                    A(HN[:, i, :], N_[:, 129 * i:129 * i + P], ACT.Copy, scale=SMALL[:, 36 + i:37 + i])\
                        .then_inc(hn_ready, 1)

            for u in range(1, U_OUT):
                split_hi(u + 1)
                if u == 3:
                    act.wait_ge(colT_read, 2)
                    act.wait_ge(consts, 4)
                for i in range(6):
                    evac(u, i)
                    part, p = gap_pair(u, i)
                    if part == 0:
                        decay_and_v(p)
                    elif part == 2:
                        divide(p)
            for i, g in enumerate((3, 2, 1, 0)):
                for b in range(NBLK):
                    act.wait_ge(mixed, 3 * i + b + 1)
                    A(Y[:, g, blk(b)], bank[b][:, 0:BLK], ACT.Copy, scale=CST[:, PS + g:PS + g + 1]).then_inc(mixed_read, 1)
            act.wait_ge(mixed_read, 12)
            act.wait_ge(y_ready, NPAIR)
            act.wait_ge(smp_y, 1)
            for b in range(NBLK):
                A(XH[:, :, blk(b)], Y[:, :, blk(b)], ACT.Copy).then_inc(cat_hi, 1)

            def mix_evac(u, f):
                b, j = (u - U_OUT) // 4, (u - U_OUT) % 4
                n = N_PROJ + 2 * (u - U_OUT) + f
                act.wait_ge(gemm_done, n + 1)
                if f == 0 and j == 0:
                    act.wait_ge(cat_lo, b + 1)
                A(Y[:, 2 * j + f, blk(b)], bank[n % 3][:, 0:BLK], ACT.Copy).then_inc(gemm_read, 1)

            def ln1_sqrt(t):
                n, q = TILES[t][1], t % 2
                act.wait_ge(ln_dve, 4 * t + 2)
                A(LNT[0:n, q, 15:16], LNT[0:n, q, 14:15], ACT.Sqrt).then_inc(ln_sqrt, 1)

            def x1_T(t):
                n = TILES[t][1]
                act.wait_ge(nT_ready, t + 1)
                if t:
                    act.wait_ge(x1_acc, t)
                else:
                    act.wait_ge(vm_ready, 8)
                    act.wait_ge(outer_ready, 8)
                for f in range(KC):
                    A(XV[:, f, 0:n], (T_, D_)[f // 4][:, P * (f % 4):P * (f % 4) + n], ACT.Identity,
                      scale=CST[:, G1 + f:G1 + f + 1], bias=CST[:, B1 + f:B1 + f + 1]).then_inc(xv_ready, 1)

            for u in range(U_OUT, U_FFN):
                b, j = (u - U_OUT) // 4, (u - U_OUT) % 4
                if u + 1 < U_FFN:
                    split_hi(u + 1)
                mix_evac(u, 0)
                if u == U_OUT:
                    act.wait_ge(nat_T, 1)
                    A(UN[0:NBUF + NS, :], B_[0:NBUF + NS, :], ACT.Copy).then_inc(nat_read, 1)
                    act.wait_ge(kvs_T, 1)
                    A(KVN[0:32, :, :], T_[0:32, 0:256].rearrange("p (i n) -> p i n", i=2), ACT.Copy).then_inc(kvs_read, 1)
                    act.wait_ge(nat_T, 2)
                    A(NN[0:36, :], D_[0:36, 0:P], ACT.Copy).then_inc(nat_read, 1)
                if b:
                    t = 3 * (b - 1) + j
                    if j < 3:
                        ln1_sqrt(t)
                    if j >= 1:
                        x1_T(t - 1)
                mix_evac(u, 1)

            for t in range(6, 9):
                ln1_sqrt(t)
                if t > 6:
                    x1_T(t - 1)
            x1_T(8)
            act.wait_ge(state_out, 16 * NH)

            with act.Fori(0, NG) as g:

                def ffn_hi(i):
                    s = U_FFN + i
                    act.wait_ge(raw_in[s % 2], g * 32 + ffn_raw(i))
                    if i < 2:
                        act.wait_ge(down_done, g * 24 + 12 * (i + 1))
                    else:
                        act.wait_ge(gemm_done, g * 12 + (N_OUT + 6 * (i - 1)))
                    A(WH[:, s % 2, :], RAW[:, s % 2, :], ACT.Copy).then_inc(hi_done, 1)

                def hidden(i):
                    n = N_OUT + i
                    c = 2 * (i // 6) + i % 2
                    act.wait_ge(gemm_done, g * 12 + (n + 1))
                    act.wait_ge(h_hi, g * 12 + (i + 1))
                    A(RT[:, i % 2, :], bank[n % 3][:, 0:BLK], ACT.Relu,
                      bias=SMALL[:, 4 + c:5 + c]).then_inc(gemm_read, 1)
                    act.wait_ge(gemm_read, g * 12 + (n + 1))
                    act.wait_ge(h_lo, g * 12 + (i + 1))
                    A(SQ[:, i % 2, :], RT[:, i % 2, :], ACT.Square).then_inc(sq_done, 1)

                A(SMALL[:, 4:8], CST[:, bass.ds(g * 4 + BF, 4)], ACT.Copy).then_inc(bf_ready, 1)
                ffn_hi(0)
                ffn_hi(1)
                act.wait_ge(bf_ready, g + 1)
                for i in range(6):
                    hidden(i)
                ffn_hi(2)
                for i in range(6, 12):
                    hidden(i)
                ffn_hi(3)
            for t, (t0, n) in enumerate(TILES):
                q = t % 2
                act.wait_ge(l2_dve, 4 * t + 2)
                A(LNT[0:n, q, 15:16], LNT[0:n, q, 14:15], ACT.Sqrt).then_inc(l2_sqrt, 1)
                act.wait_ge(l2_dve, 4 * t + 4)
                if t >= 3:
                    act.wait_ge(out_done[t % 3], 16 * (t // 3))
                for half in range(2):
                    A(OUT[t % 3][0:n, 512 * half:512 * (half + 1)], bank[(6, 0)[q] + half][0:n, :], ACT.Identity,
                      bias=LNT[0:n, q, 17:18], scale=LNT[0:n, q, 16:17]).then_inc(l2_norm, 1)

        @block.vector
        def _(dve):
            V = nc.vector
            stt = V.scalar_tensor_tensor

            def split_lo(u):
                dve.wait_ge(hi_done, u + 1)
                if u == 0:
                    raw, hi, lo = wslot(RAW, 0), gslot(WH).bitcast(F32), gslot(WL)
                    V.tensor_tensor(lo[:, :, 0:NH], raw[:, :, 0:NH], hi[:, :, 0:NH], ALU.subtract)
                    V.tensor_tensor(lo[:, :, 32:32 + NH], raw[:, :, NH:2 * NH], hi[:, :, 32:32 + NH],
                                    ALU.subtract).then_inc(lo_done, 1)
                else:
                    V.tensor_tensor(WL[:, u % 2, :], RAW[:, u % 2, :], WH[:, u % 2, :].bitcast(F32),
                                    ALU.subtract).then_inc(lo_done, 1)

            row_n = [0]

            def row(ins, value=None):
                row_n[0] += 1
                ins.then_inc(dve_row, 1)
                assert value in (None, row_n[0]), (value, row_n[0])

            def after_rows():
                dve.wait_ge(dve_row, row_n[0])

            V.memset(WL[:, 0, 0:KC * GATE_ROWS].bitcast(F32), 0.0)
            row(V.memset(WH[:, 0, 0:KC * GATE_ROWS].bitcast(F32), 0.0), ROW_PAD)
            after_rows()
            for j in range(NBUF - 1):
                V.memset(INV[:, j:j + 1], 1.0 / (j + 1))
            V.memset(INV[:, NBUF - 1:NBUF], 1.0 / NBUF)
            V.memset(RBH[:, :].bitcast(F32), 0.0)
            row(V.memset(RBL[:, :].bitcast(F32), 0.0), ROW_INV)
            for s in range(2 * len(TILES)):
                t0, n = TILES[s // 2]
                ks = slice(4 * (s % 2), 4 * (s % 2) + 4)
                dve.wait_ge(x_hi, s + 1)
                V.tensor_tensor(XL[:, ks, t0:t0 + n],
                                bank[3 + s % 4][:, :].rearrange("p (k n) -> p k n", k=4)[:, :, 0:n],
                                XH[:, ks, t0:t0 + n].bitcast(F32), ALU.subtract).then_inc(x_lo, 1)
                if s == 5:
                    split_lo(0)
                elif s == 11:
                    split_lo(1)
            dve.wait_ge(stT_read, 2)
            for g, w in enumerate(WINDOWS):
                V.tensor_reduce(WSUM[:, g, :], SPT[:, g, :, NBUF - (w - 1):NBUF], AX.X, ALU.add).then_inc(wsum_ready, 1)

            def chunks(t):
                return t[0:NH, pr].rearrange("h (c t) -> h c t", t=P)

            dve.wait_ge(act_row, 3)
            row(stt(TF[0:NH, :], TF[0:NH, :], 0.0, TZ[0:NH, :], ALU.min, ALU.subtract))
            dve.wait_ge(consts, 6)
            dve.wait_ge(bias_in, 16 * 3)
            after_rows()
            V.tensor_tensor_scan(TBS[0:NH, pr], TN[0:NH, pr], TF[0:NH, pr], 0.0, ALU.mult, ALU.add)
            V.tensor_tensor_scan(TM[0:NH, pr], TF[0:NH, pr], TI[0:NH, pr], 0.0, ALU.add, ALU.max)
            row(V.tensor_tensor(SMALL[0:NH, 16:24], TF[0:NH, sa], SMALL[0:NH, 8:16], ALU.add))
            after_rows()
            row(V.tensor_tensor(TM[0:NH, sa], SMALL[0:NH, 16:24], TI[0:NH, sa], ALU.max))
            after_rows()
            V.tensor_copy(SMALL[0:NH, 40:49], TM[0:NH, SEQ - 1:NT])
            V.memset(SMALL[0:NH, 24:25], 0.0)
            row(V.tensor_copy(SMALL[0:NH, 25:32], chunks(TM)[:, 0:NCH - 1, P - 1]), ROW_M)
            row(V.tensor_tensor(TN[0:NH, pr], TBS[0:NH, pr], TM[0:NH, pr], ALU.subtract), ROW_NEGM)
            after_rows()
            V.tensor_tensor(chunks(TZ), chunks(TN), SMALL[0:NH, 24:32].rearrange("h (c o) -> h c o", o=1)
                            .to_broadcast([NH, NCH, P]), ALU.add)
            row(V.tensor_tensor(TZ[0:NH, sa], SMALL[0:NH, 16:24], TM[0:NH, sa], ALU.subtract), ROW_Z)
            row(V.tensor_tensor(RC[0:NH, pr], TI[0:NH, pr], TBS[0:NH, pr], ALU.subtract), ROW_A)
            after_rows()
            V.tensor_tensor(chunks(TBS), chunks(RC), chunks(TN)[:, :, P - 1:P].to_broadcast([NH, NCH, P]), ALU.add)
            row(V.tensor_tensor(TBS[0:NH, sa], TI[0:NH, sa], TM[0:NH, sa], ALU.subtract), ROW_W)
            dve.wait_ge(act_row, 8)
            V.tensor_tensor(RBL[0:NH, pr], TN[0:NH, pr], RBH[0:NH, pr].bitcast(F32), ALU.subtract)
            row(V.tensor_tensor(RBL[32:32 + NH, :], RC[32:32 + NH, :], RBH[32:32 + NH, :].bitcast(F32),
                                ALU.subtract), ROW_LO)
            last_of_chunk = RC[:, pr].rearrange("p (o c t) -> p o c t", o=1, t=P)[:, :, :, P - 1]
            of_samples = RC[:, sa].rearrange("p (o c) -> p o c", o=1)
            for i, (g, src) in enumerate(((1, last_of_chunk), (1, of_samples), (2, of_samples), (3, of_samples))):
                onehot = IDN[:, 32 * g:32 * g + NH].rearrange("p (h o) -> p h o", o=1).to_broadcast([P, NH, NS])
                ins = V.tensor_tensor(ST[:, i, :, :], src.to_broadcast([P, NH, NS]), onehot, ALU.mult)
            row(ins, ROW_RX)

            def gate_columns():
                for i in range(2):
                    dve.wait_ge(colT, i + 1)
                    V.tensor_copy(COLS[:, 4 * i:4 * i + 4, :, :],
                                  (T_, D_)[i][:, :].rearrange("p (c g r) -> p c g r", c=4, g=4)[:, :, :, 0:NH])\
                        .then_inc(colT_read, 1)
                dve.wait_ge(colT, 3)
                V.tensor_copy(BC[:, :, :, :].rearrange("p k h b -> p (k h b)"), N_[:, 0:P]).then_inc(colT_read, 1)

            def gate_h(p):
                h, j, cs = pair(p)
                dve.wait_ge(s_ready, p + 2)
                V.tensor_tensor(Y[:, 4 + h, cs], S_[:, 256:512], Y[:, 4 + h, cs], ALU.mult).then_inc(y_ready, 1)

            def att1(p):
                h, j, cs = pair(p)
                dve.wait_ge(E_ready, 2 * (p + 1))
                if p:
                    dve.wait_ge(num_ready, p)
                V.tensor_tensor(QI[:, :, :].rearrange("p i n -> p (i n)"), QKV[h % 2][:, 0, cs], B_[:, 256:512],
                                ALU.mult).then_inc(qi_ready, 1)
                dve.wait_ge(v_ready, p + 1)
                V.tensor_tensor(KW[:, :, :], T_[:, 0:256].rearrange("p (i n) -> p i n", i=2),
                                COLS[:, 2 * j:2 * j + 2, 2, h:h + 1].to_broadcast([P, 2, P]), ALU.mult).then_inc(kw_ready, 1)
                dve.wait_ge(s_ready, p + 1)
                dve.wait_ge(Em_ready, p + 1)
                V.tensor_tensor(PT[:, :, :].rearrange("p i n -> p (i n)"), S_[:, 0:256],
                                E[:, :, :].rearrange("p i n -> p (i n)"), ALU.mult).then_inc(P_ready, 1)
                if p:
                    gate_h(p - 1)

            def att2(p):
                h, j, _ = pair(p)
                dve.wait_ge(dC_ready, p + 1)
                for i in range(2):
                    c = 2 * j + i
                    new, old, d = CA[:, (c + 1) % 3, :], CA[:, c % 3, :], D_[:, 129 * i:129 * (i + 1)]
                    if c == 0:
                        V.tensor_copy(new, d).then_inc(C_ready, 1)
                    else:
                        if c == 1 and h:
                            dve.wait_ge(state_out, 16 * h)
                        dve.wait_ge(C_ready, NCH * h + c)
                        stt(new, old, BC[:, 0, h, c:c + 1], d, ALU.mult, ALU.add).then_inc(C_ready, 1)

            def att3(p):
                h, j, _ = pair(p)
                dve.wait_ge(num_ready, p + 1)
                den = N_[:, 0:258].rearrange("p (i n) -> p i n", i=2)[:, :, DH]
                V.tensor_tensor(SMALL[:, 32:34], den, COLS[:, 2 * j:2 * j + 2, 3, h], ALU.max).then_inc(den_ready, 1)
                dve.wait_ge(den_ready, 2 * p + 1)
                stt(SMALL[:, 34:36], den, -1.0, SMALL[:, 32:34], ALU.mult, ALU.max).then_inc(den_ready, 1)
                dve.wait_ge(den_ready, 2 * p + 2)
                if p:
                    dve.wait_ge(hn_ready, 2 * p)
                if p >= NPAIR - NH:
                    V.tensor_copy(ST[:, 7, p - (NPAIR - NH), :], N_[:, 264:264 + NS])
                if p == NPAIR - NH:
                    V.tensor_copy(ST[:, 5:7, :, :].rearrange("p a h b -> p (a h b)"), N_[:, 300:364])
                V.reciprocal(SMALL[:, 36:38], SMALL[:, 34:36]).then_inc(r_ready, 1)
                if j == PAIRS - 1:
                    dve.wait_ge(C_ready, NCH * (h + 1))
                    V.tensor_copy(NO[:, 32 + h:33 + h], CA[:, NCH % 3, DH:DH + 1]).then_inc(ncol_ready, 1)

            win_n = [0]

            def win(ins):
                win_n[0] += 1
                ins.then_inc(win_step, 1)
                dve.wait_ge(win_step, win_n[0])

            def window(g, n_out):
                w = WINDOWS[g]
                u = Y[:, g, :]
                dve.wait_ge(gemm_read, n_out)
                V.tensor_copy(US[:, g, :], u[:, SEQ - NBUF:NT])
                V.tensor_copy(TA[:, 8:9], u[:, 0:1])
                V.tensor_tensor(ST[:, 9, 0, :], WSUM[:, g, :], u[:, sa], ALU.add)
                win(V.tensor_tensor(TA[:, 9:8 + SEQ], u[:, 1:SEQ], u[:, 0:SEQ - 1], ALU.add))
                src, dst, d = TA, TB, 2
                while d < w:
                    win(V.tensor_tensor(dst[:, 8:8 + SEQ], src[:, 8:8 + SEQ], src[:, 8 - d:8 - d + SEQ], ALU.add))
                    src, dst, d = dst, src, 2 * d
                win(V.tensor_tensor(TAIL[:, 0:w - 1], src[:, 8:8 + w - 1], INV[:, 0:w - 1], ALU.mult))
                win(V.tensor_tensor(TAIL[:, 0:w - 1], TAIL[:, 0:w - 1], u[:, 0:w - 1], ALU.subtract))
                V.tensor_copy(u[:, 0:w - 1], TAIL[:, 0:w - 1])
                stt(u[:, w - 1:SEQ], src[:, 8 + w - 1:8 + SEQ], 1.0 / w, u[:, w - 1:SEQ], ALU.mult, ALU.subtract)
                stt(u[:, sa], ST[:, 9, 0, :], 1.0 / w, u[:, sa], ALU.mult, ALU.subtract).then_inc(pooled, 1)

            smp_c = [0]

            def step(ins):
                smp_c[0] += 1
                ins.then_inc(smp, 1)
                dve.wait_ge(smp, smp_c[0])

            q_s, k_s, v_s = SM[:, 0, :, :], SM[:, 1, :, :], SM[:, 2, :, :]
            iw_s, dw_s, em_s = BC[:, 1, :, :], BC[:, 2, :, :], BC[:, 3, :, :]
            for u in range(1, U_OUT):
                split_lo(u + 1)
                if u == 2:
                    gate_columns()
                    dve.wait_ge(colT_read, 3)
                    dve.wait_ge(wsum_ready, 4)
                if u == 9:
                    dve.wait_ge(smp_kept, 3 * NH)
                    V.tensor_tensor(ST[:, 0, :, :], q_s, k_s, ALU.mult)
                    step(V.tensor_tensor(ST[:, 2, :, :], q_s, iw_s, ALU.mult))
                    V.tensor_tensor(ST[:, 1, :, :], n0T, ST[:, 2, :, :], ALU.mult).then_inc(prod_ready, 1)
                    V.memset(TA[:, 0:8], 0.0)
                    win(V.memset(TB[:, 0:8], 0.0))
                for i in range(6):
                    part, p = gap_pair(u, i)
                    if part is not None:
                        (att1, att2, att3)[part](p)
                    if u >= 9 and i in (3, 5):
                        window(UCH[u, i // 4], N_GATE + 6 * (u - 1) + (3 if i == 3 else 6))
            gate_h(NPAIR - 1)

            s_, nq, num = ST[:, 5, :, :], ST[:, 6, :, :], ST[:, 7, :, :]
            step(V.tensor_tensor(s_, s_, dw_s, ALU.mult))
            V.tensor_tensor(ST[:, 3, :, :], s_, v_s, ALU.mult)
            step(V.tensor_tensor(nq, nq, s_, ALU.add))
            V.tensor_tensor(num, num, ST[:, 3, :, :], ALU.add)
            step(V.tensor_tensor(ST[:, 4, :, :], nq, em_s, ALU.max))
            step(stt(nq, nq, -1.0, ST[:, 4, :, :], ALU.mult, ALU.max))
            step(V.reciprocal(ST[:, 4, :, :], nq))
            step(V.tensor_tensor(num, num, ST[:, 4, :, :], ALU.mult))
            V.tensor_tensor(Y[:, 4:8, sa], Y[:, 4:8, sa], num, ALU.mult).then_inc(smp_y, 1)
            V.tensor_tensor(ST[:, 0, :, :], k_s, dw_s, ALU.mult)
            V.tensor_tensor(ST[:, 8, :, :], v_s, dw_s, ALU.mult).then_inc(smp_n, 1)
            NO_s = NO[:, 0:32].rearrange("p (h b) -> p h b", h=NH)
            step(V.tensor_tensor(NO_s, n0T, iw_s, ALU.mult))
            V.tensor_tensor(NO_s, NO_s, ST[:, 0, :, :], ALU.add).then_inc(smp_n, 1)
            for b in range(NBLK):
                dve.wait_ge(cat_hi, b + 1)
                V.tensor_tensor(XL[:, :, blk(b)], Y[:, :, blk(b)], XH[:, :, blk(b)].bitcast(F32),
                                ALU.subtract).then_inc(cat_lo, 1)

            def vmask(i):
                dve.wait_ge(kvs_read, 1)
                if i >= 2:
                    dve.wait_ge(outer_ready, i - 1)
                V.tensor_tensor(VM[0:32, i % 2, :, :], KVN[0:32, 1:2, :].to_broadcast([32, 4, P]),
                                IDN[0:32, 4 * i:4 * i + 4].rearrange("p (a o) -> p a o", o=1).to_broadcast([32, 4, P]),
                                ALU.mult).then_inc(vm_ready, 1)

            def new_C(i):
                dve.wait_ge(outer_ready, i + 1)
                for x in range(4):
                    h, s = (4 * i + x) // NS, (4 * i + x) % NS
                    stt(C0[:, h, s, :], C0[:, h, s, :], BC[:, 1, h, s:s + 1], (B_, N_)[i % 2][:, P * x:P * (x + 1)],
                        ALU.mult, ALU.add).then_inc(C_new, 1)

            def layer_norm_numbers(x0, x1, t, done, mid, sqrt_done):
                L = LNT[0:TILES[t][1], t % 2, :]
                V.bn_stats(L[:, 0:6], x0)
                V.bn_stats(L[:, 6:12], x1).then_inc(done, 1)
                dve.wait_ge(done, 4 * t + 1)
                V.bn_aggr(L[:, 12:14], L[:, 0:12]).then_inc(mid, 1)
                dve.wait_ge(mid, t + 1)
                V.tensor_scalar(L[:, 14:15], L[:, 13:14], EPS, None, ALU.add).then_inc(done, 1)
                dve.wait_ge(sqrt_done, t + 1)
                V.reciprocal(L[:, 16:17], L[:, 15:16]).then_inc(done, 1)
                dve.wait_ge(done, 4 * t + 3)
                stt(L[:, 17:18], L[:, 12:13], -1.0, L[:, 16:17], ALU.mult, ALU.mult).then_inc(done, 1)

            def ln1_a(t):
                n, q = TILES[t][1], t % 2
                dve.wait_ge(xn_in[q], arrived(t, 2))
                dve.wait_ge(mixT_ready, t + 1)
                if t >= 2:
                    dve.wait_ge(nT_ready, t - 1)
                for half in range(2):
                    cs = slice(512 * half, 512 * (half + 1))
                    last = stt(RS[0:n, q, cs], XN[0:n, q, cs], ALPHA, (B_, S_)[half][0:n, :], ALU.mult, ALU.add)
                last.then_inc(res_done, 1)
                dve.wait_ge(res_done, t + 1)
                layer_norm_numbers(RS[0:n, q, 0:512], RS[0:n, q, 512:1024], t, ln_dve, ln_aggr, ln_sqrt)

            def ln1_b(t):
                t0, n = TILES[t]
                dve.wait_ge(x1_hi, t + 1)
                V.tensor_tensor(XL[:, :, t0:t0 + n], XV[:, :, 0:n], XH[:, :, t0:t0 + n].bitcast(F32),
                                ALU.subtract).then_inc(x1_lo, 1)
                stt(Y[:, :, t0:t0 + n], XV[:, :, 0:n], ALPHA, CST[:, B2:B2 + 8].rearrange("p (k o) -> p k o", o=1)
                    .to_broadcast([P, KC, n]), ALU.mult, ALU.add).then_inc(x1_acc, 1)

            for u in range(U_OUT, U_FFN):
                b, j = (u - U_OUT) // 4, (u - U_OUT) % 4
                if u + 1 < U_FFN:
                    split_lo(u + 1)
                if b == 0:
                    for i in (2 * j, 2 * j + 1):
                        vmask(i)
                        new_C(i)
                else:
                    t = 3 * (b - 1) + j
                    if j < 3:
                        ln1_a(t)
                    if j >= 1:
                        ln1_b(t - 1)
            for t in range(6, 9):
                ln1_a(t)
                if t > 6:
                    ln1_b(t - 1)
            ln1_b(8)
            dve.wait_ge(x1_acc, 9)
            dve.sem_inc(h_hi, 2)
            dve.sem_inc(h_lo, 2)
            dve.sem_inc(down_read, 3)

            with dve.Fori(0, NG) as g:

                def ffn_lo(i):
                    s = U_FFN + i
                    dve.wait_ge(hi_done, g * 4 + (s + 1))
                    V.tensor_tensor(WL[:, s % 2, :], RAW[:, s % 2, :], WH[:, s % 2, :].bitcast(F32),
                                    ALU.subtract).then_inc(lo_done, 1)

                def hidden(i):
                    c, b = 2 * (i // 6) + i % 2, i % 6 // 2
                    dve.wait_ge(sq_done, g * 12 + (i + 1))
                    V.tensor_tensor(HH[:, c, blk(b)], RT[:, i % 2, :], RT[:, i % 2, :], ALU.mult).then_inc(h_hi, 1)
                    dve.wait_ge(h_hi, g * 12 + (i + 3))
                    V.tensor_tensor(HL[:, c, blk(b)], SQ[:, i % 2, :], HH[:, c, blk(b)].bitcast(F32),
                                    ALU.subtract).then_inc(h_lo, 1)

                def add_down(i):
                    o, b = 4 * (i // 12) + i % 4, i % 12 // 4
                    dve.wait_ge(down_done, g * 24 + (24 + i + 1))
                    V.tensor_tensor(Y[:, o, blk(b)], Y[:, o, blk(b)], bank[3 + i % 3][:, 0:BLK], ALU.add).then_inc(down_read, 1)

                ffn_lo(0)
                ffn_lo(1)
                for i in range(6):
                    hidden(i)
                ffn_lo(2)
                for i in range(6, 12):
                    hidden(i)
                ffn_lo(3)
                for i in range(24):
                    add_down(i)

            def scale2(t):
                n = TILES[t][1]
                dve.wait_ge(l2_norm, 2 * t + 2)
                V.tensor_tensor(OUT[t % 3][0:n, :], OUT[t % 3][0:n, :], GB[0:n, 0, :], ALU.mult).then_inc(l2_g, 1)

            dve.wait_ge(gb_in, 32)
            for t in range(len(TILES)):
                n, q = TILES[t][1], t % 2
                dve.wait_ge(l2_T, t + 1)
                if t >= 2:
                    dve.wait_ge(l2_norm, 2 * (t - 1))
                layer_norm_numbers(bank[(6, 0)[q]][0:n, :], bank[(6, 0)[q] + 1][0:n, :], t, l2_dve, l2_aggr, l2_sqrt)
                if t:
                    scale2(t - 1)
            scale2(len(TILES) - 1)

        @block.tensor
        def _(pe):
            def mm(out, lhsT, rhs, start=True, stop=True):
                return nc.tensor.matmul(out, lhsT, rhs, start=start, stop=stop, skip_group_check=True)

            def tr(out, in_):
                n = in_.shape[0]
                return nc.tensor.transpose(out, in_, IDN[0:n, 0:n])

            def split_product(out, w_hi, w_lo, x_hi_, x_lo_, nk):
                for k in range(nk):
                    mm(out, w_hi(k), x_hi_(k), k == 0, False)
                    mm(out, w_hi(k), x_lo_(k), False, False)
                    last = mm(out, w_lo(k), x_hi_(k), False, k == nk - 1)
                return last

            pe.wait_ge(consts, 1)
            for s in range(2 * len(TILES)):
                t, half = s // 2, s % 2
                n = TILES[t][1]
                if s % 6 == 0:
                    pe.wait_ge(x_in[s // 6], 16 * (3 + (s == 12)))
                if s >= 4:
                    pe.wait_ge(x_lo, s - 3)
                for k in range(4):
                    last = tr(bank[3 + s % 4][:, P * k:P * k + n], XNAT[0:n, t, P * (4 * half + k):P * (4 * half + k + 1)])
                last.then_inc(xT_ready, 1)
            pe.wait_ge(small_in, 16 * 8)
            pe.wait_ge(x_lo, 2 * len(TILES))
            tr(B_[:, 0:92], CN[0:92, :]).then_inc(stT_ready, 1)
            for g in range(4):
                last = tr(S_[:, P * g:P * g + NS * NBUF], SPN[0:NS * NBUF, P * g:P * (g + 1)])
            last.then_inc(stT_ready, 1)

            pe.wait_ge(lo_done, 1)
            for b in range(NBLK):
                split_product(bank[b][0:GATE_ROWS, 0:BLK], lambda k: gslot(WH)[:, k, :], lambda k: gslot(WL)[:, k, :],
                              lambda k: XH[:, k, blk(b)], lambda k: XL[:, k, blk(b)], KC).then_inc(gemm_done, 1)

            def unit_product(u, f, b, n):
                pe.wait_ge(gemm_read, n - 2)
                cs = slice(P * f, P * (f + 1))
                return split_product(bank[n % 3][:, 0:BLK], lambda k: wslot(WH, u)[:, k, cs], lambda k: wslot(WL, u)[:, k, cs],
                                     lambda k: XH[:, k, blk(b)], lambda k: XL[:, k, blk(b)], KC)

            def att1(p):
                if p:
                    pe.wait_ge(hn_ready, 2 * p)
                    pe.wait_ge(P_ready, p)
                    if p >= 2:
                        pe.wait_ge(y_ready, p - 1)
                    for i in range(2):
                        last = tr(S_[:, 256 + P * i:256 + P * (i + 1)], HN[:, i, :])
                    if p == NPAIR:
                        last.then_inc(s_ready, 1)
                        return
                    pe.wait_ge(qi_ready, p)
                    pe.wait_ge(kw_ready, p)
                h, j, cs = pair(p)
                kT, qT, vT = QKV[h % 2][:, 1, :], QKV[h % 2][:, 0, :], QKV[h % 2][:, 2, :]
                for g in range(2):
                    mm(B_[:, 256 * g:256 * (g + 1)], SEL[:, g, h, :], RBH[:, cs], True, False)
                    last = mm(B_[:, 256 * g:256 * (g + 1)], SEL[:, g, h, :], RBL[:, cs], False, True)
                last.then_inc(bc_ready, 1)
                for i in range(2):
                    c = slice(P * (2 * j + i), P * (2 * j + i + 1))
                    last = mm(S_[:, P * i:P * (i + 1)], kT[:, c], qT[:, c])
                last.then_inc(s_ready, 1)
                for x, src in enumerate((kT, vT)):
                    for i in range(2):
                        c = slice(P * (2 * j + i), P * (2 * j + i + 1))
                        last = tr(T_[:, 256 * x + P * i:256 * x + P * (i + 1)], src[:, c])
                last.then_inc(kvT_ready, 1)

            def att2(p):
                pe.wait_ge(kw_ready, p + 1)
                if p:
                    pe.wait_ge(C_ready, 2 * p)
                for i in range(2):
                    last = mm(D_[:, 129 * i:129 * (i + 1)], KW[:, i, :], VA[:, i, :])
                last.then_inc(dC_ready, 1)

            def att3(p):
                h, j, _ = pair(p)
                pe.wait_ge(P_ready, p + 1)
                pe.wait_ge(qi_ready, p + 1)
                pe.wait_ge(C_ready, 2 * p + 1)
                if p:
                    pe.wait_ge(hn_ready, 2 * p)
                for i in range(2):
                    c = 2 * j + i
                    out = N_[:, 129 * i:129 * (i + 1)]
                    last = mm(out, PT[:, i, :], VA[:, i, :], True, c == 0)
                    if c:
                        last = mm(out, QI[:, i, :], CA[:, c % 3, :], False, True)
                if p >= NPAIR - NH:
                    s = p - (NPAIR - NH)
                    if s == 0:
                        pe.wait_ge(c_in, 16 * NH)
                        pe.wait_ge(prod_ready, 1)
                        mm(N_[:, 300:364], ONES[:, :], ST[:, 0:2, :, :].rearrange("p a h b -> p (a h b)"))
                    for b in range(NS):
                        last = mm(N_[:, 264 + b:265 + b], C0[:, s, b, :], ST[:, 2, s, b:b + 1])
                last.then_inc(num_ready, 1)

            for u in range(1, U_OUT):
                pe.wait_ge(lo_done, u + 1)
                if u == 2:
                    pe.wait_ge(dve_row, ROW_RX)
                    pe.wait_ge(stT_read, 2)
                    for i in range(2):
                        for c in range(4):
                            last = tr((T_, D_)[i][:, P * c:P * (c + 1)], RC[:, P * (4 * i + c):P * (4 * i + c + 1)])
                        last.then_inc(colT, 1)
                    mm(N_[:, 0:P], ONES[:, :], ST[:, 0:4, :, :].rearrange("p a h b -> p (a h b)")).then_inc(colT, 1)
                if u == 3:
                    pe.wait_ge(colT_read, 3)
                    pe.wait_ge(consts, 4)
                for i in range(6):
                    n = N_GATE + 6 * (u - 1) + i
                    f = UCH[u, i // 3] % 2 if u >= 9 else i // 3
                    unit_product(u, f, i % 3, n).then_inc(gemm_done, 1)
                    part, p = gap_pair(u, i)
                    if part is not None:
                        (att1, att2, att3)[part](p)
            att1(NPAIR)

            for i, g in enumerate((3, 2, 1, 0)):
                pe.wait_ge(pooled, i + 1)
                for b in range(NBLK):
                    if i == 0:
                        pe.wait_ge(gemm_read, N_PROJ - 2 + b)
                    else:
                        pe.wait_ge(mixed_read, 3 * (i - 1) + b + 1)
                    mm(bank[b][:, 0:BLK], WP[:, g, :], Y[:, g, blk(b)]).then_inc(mixed, 1)

            def outer(i):
                pe.wait_ge(vm_ready, i + 1)
                if i >= 2:
                    pe.wait_ge(C_new, 4 * (i - 1))
                mm((B_, N_)[i % 2][:, :], KVN[0:32, 0, :],
                   VM[0:32, i % 2, :, :].rearrange("p a n -> p (a n)")).then_inc(outer_ready, 1)

            def mix_T(t):
                t0, n = TILES[t]
                pe.wait_ge(gemm_read, N_PROJ + KC * (t // 3 + 1))
                if t:
                    pe.wait_ge(res_done, t)
                else:
                    pe.wait_ge(C_new, 32)
                for f in range(KC):
                    last = tr((B_, S_)[f // 4][0:n, P * (f % 4):P * (f % 4 + 1)], Y[:, f, t0:t0 + n])
                last.then_inc(mixT_ready, 1)

            def norm_T(t):
                t0, n = TILES[t]
                pe.wait_ge(ln_norm, t + 1)
                if t:
                    pe.wait_ge(xv_ready, KC * t)
                for f in range(KC):
                    last = tr((T_, D_)[f // 4][:, P * (f % 4):P * (f % 4) + n], RS[0:n, t % 2, P * f:P * (f + 1)])
                last.then_inc(nT_ready, 1)

            for u in range(U_OUT, U_FFN):
                b, j = (u - U_OUT) // 4, (u - U_OUT) % 4
                pe.wait_ge(lo_done, u + 1)
                if j == 0:
                    pe.wait_ge(cat_lo, b + 1)
                for f in range(2):
                    n = N_PROJ + 2 * (u - U_OUT) + f
                    unit_product(u, f, b, n).then_inc(gemm_done, 1)
                    if b == 0:
                        if u == U_OUT and f == 0:
                            for g in range(4):
                                last = tr(B_[0:NBUF + NS, P * g:P * (g + 1)], US[:, g, :])
                            last.then_inc(nat_T, 1)
                            pe.wait_ge(smp_n, 2)
                            pe.wait_ge(ncol_ready, NH)
                            tr(T_[0:32, 0:P], SM[:, 1, :, :].rearrange("p h b -> p (h b)"))
                            tr(T_[0:32, P:2 * P], ST[:, 8, :, :].rearrange("p h b -> p (h b)")).then_inc(kvs_T, 1)
                            tr(D_[0:36, 0:P], NO[:, :]).then_inc(nat_T, 1)
                            pe.wait_ge(nat_read, 1)
                        outer(2 * j + f)
                    elif f == 0:
                        t = 3 * (b - 1) + j
                        if j >= 1:
                            norm_T(t - 1)
                        if j < 3:
                            mix_T(t)
            mix_T(6)
            norm_T(6)
            mix_T(7)
            norm_T(7)
            mix_T(8)
            norm_T(8)
            pe.wait_ge(x1_lo, 9)
            pe.sem_inc(down_done, 24)

            with pe.Fori(0, NG) as g:
                for i in range(2):
                    s = U_FFN + i
                    pe.wait_ge(lo_done, g * 4 + (s + 1))
                    for b in range(NBLK):
                        for f in range(2):
                            n = N_OUT + 6 * i + 2 * b + f
                            pe.wait_ge(gemm_read, g * 12 + (n - 2))
                            cs = slice(P * f, P * (f + 1))
                            split_product(bank[n % 3][:, 0:BLK], lambda k: wslot(WH, s)[:, k, cs],
                                                 lambda k: wslot(WL, s)[:, k, cs], lambda k: XH[:, k, blk(b)],
                                                 lambda k: XL[:, k, blk(b)], KC).then_inc(gemm_done, 1)
                for i in range(2):
                    s = U_FFN + 2 + i
                    pe.wait_ge(lo_done, g * 4 + (s + 1))
                    for b in range(NBLK):
                        if i == 0:
                            pe.wait_ge(h_lo, g * 12 + (2 + 6 + 2 * b + 2))
                        for o in range(4):
                            m = 12 * i + 4 * b + o
                            pe.wait_ge(down_read, g * 24 + (m + 1))
                            cs = slice(P * o, P * (o + 1))
                            split_product(bank[3 + m % 3][:, 0:BLK], lambda k: wslot2(WH, s)[:, k, cs],
                                                 lambda k: wslot2(WL, s)[:, k, cs], lambda k: HH[:, k, blk(b)],
                                                 lambda k: HL[:, k, blk(b)], FG // P).then_inc(down_done, 1)

            pe.wait_ge(down_read, 3 + 24 * NG)
            for t, (t0, n) in enumerate(TILES):
                q = t % 2
                if t >= 2:
                    pe.wait_ge(l2_norm, 2 * (t - 1))
                for f in range(KC):
                    last = tr(bank[(6, 0)[q] + f // 4][0:n, P * (f % 4):P * (f % 4 + 1)], Y[:, f, t0:t0 + n])
                last.then_inc(l2_T, 1)


_OUTS = [("y_prompt", (1, 1024, 1024)), ("y_sample", (8, 1, 1024)), ("pool_p", (1, 1, 15, 512)),
         ("C_p", (1, 1, 4, 128, 128)), ("n_p", (1, 1, 4, 128)), ("m_p", (1, 1, 4)), ("pool_s", (1, 8, 15, 512)),
         ("C_s", (1, 8, 4, 128, 128)), ("n_s", (1, 8, 4, 128)), ("m_s", (1, 8, 4))]


def kernel(**inputs):
    import numpy as _np
    import concourse.bacc as _bacc
    from concourse import mybir as _mybir
    from concourse.bass_utils import run_bass_kernel_spmd as _run

    nc = _bacc.Bacc("TRN2", target_bir_lowering=False, num_devices=1)
    arrays, args = {}, {}
    for name, value in inputs.items():
        x = _np.ascontiguousarray(value)
        arrays[f"in_{name}"] = x
        args[name] = nc.dram_tensor(f"in_{name}", x.shape, _mybir.dt.from_np(x.dtype), kind="ExternalInput").ap()
    for name, shape in _OUTS:
        args[name] = nc.dram_tensor(f"out_{name}", shape, _mybir.dt.float32, kind="ExternalOutput").ap()
    build_layer(nc, args)
    r = _run(nc, [arrays], core_ids=[0])
    return tuple(r.results[0][f"out_{name}"] for name, _ in _OUTS)
```

```python
from contextlib import ExitStack

import concourse.bass as bass
from concourse import mybir

F32, F32R = mybir.dt.float32, mybir.dt.float32r
ACT = mybir.ActivationFunctionType
ALU = mybir.AluOpType
AX = mybir.AxisListType

P = 128
SEQ, NS = 1024, 8
D = 1024
KC = D // P
NT = SEQ + NS
NBLK = 3
BLK = NT // NBLK
NH, DH = 4, 128
WINDOWS = (2, 4, 8, 16)
NBUF = max(WINDOWS) - 1
NCH = SEQ // P
DFF = 4 * D
FG = 512
NG = DFF // FG
UW = 256
ALPHA = 2.0 ** 0.25
EPS = 1e-5
TILES = [(BLK * b + P * j, min(P, BLK - P * j)) for b in range(NBLK) for j in range(3)]
PROJ = [("A", 0), ("B", 0), ("A", 1), ("B", 1), ("A", 2), ("B", 2), ("A", 3), ("B", 3), ("U", 1), ("U", 0)]
U_OUT = 1 + len(PROJ)
U_FFN = U_OUT + NBLK * (D // UW)
N_GATE = NBLK
N_PROJ = N_GATE + 6 * len(PROJ)
N_OUT = N_PROJ + NBLK * KC
GATE_ROWS = 36
PAIRS = NCH // 2


def build_layer(nc, a):
    ctx = ExitStack()
    with ctx:
        base = (nc.sbuf_base + 63) // 64 * 64
        R = {}

        def at(name, shape, off, dt=F32):
            size = 4
            for s in shape[1:]:
                size *= s
            R[name] = off + size
            return nc.alloc_sbuf_tensor_at(name, shape, dt, offset=base + off)

        XROW = NT * 4
        o_xh, o_xl, o_r1 = 0, KC * XROW, 2 * KC * XROW
        o_r2 = 3 * KC * XROW
        o_raw = 4 * KC * XROW
        o_wh = o_raw + 2 * KC * UW * 4
        o_wl = o_wh + 2 * KC * UW * 4
        o_att = o_wl + 2 * KC * UW * 4
        XH = at("x_hi", [P, KC, NT], o_xh, F32R)
        XL = at("x_lo", [P, KC, NT], o_xl, F32R)
        Y = at("y_acc", [P, KC, NT], o_r1)
        RAW = at("w_raw", [P, 2, KC * UW], o_raw)
        WH = at("w_hi", [P, 2, KC * UW], o_wh, F32R)
        WL = at("w_lo", [P, 2, KC * UW], o_wl, F32R)
        QKV = [at("qkv0", [P, 3, NT], o_r2 + 3 * XROW), at("qkv1", [P, 3, NT], o_r2)]
        C0 = at("sample_C", [P, NH, NS, DH], o_r2 + 3 * XROW)
        TB = at("win_b", [P, 8 + NT], o_r2 + 3 * XROW + 16384)
        HH = at("h_hi", [P, FG // P, NT], o_r2, F32R)
        HL = at("h_lo", [P, FG // P, NT], o_r2 + 4 * XROW, F32R)
        XNAT = at("x_nat_all", [P, len(TILES), D], o_r1)
        SPN = at("state_pool_nat", [P, 4 * P], o_r2 + 3 * XROW + 16384)
        CN = at("const_nat", [P, P], o_r2 + 3 * XROW + 16384 + 2048)
        SPT = at("state_pool_T", [P, 4, NS, NBUF], o_r2 + 4096)
        row = lambda name, ch: at(name, [P, NT], o_r1 + ch * XROW)
        RC = row("gate_rows", 0)
        TI, TF, TBS = row("row_i", 1), row("row_f", 2), row("row_b", 3)
        TM, TN, TZ = row("row_m", 5), row("row_negM", 6), row("row_z", 7)
        cur = [o_att]

        def put(name, shape, dt=F32):
            t = at(name, shape, cur[0], dt)
            cur[0] = (R[name] + 31) // 32 * 32
            return t

        IDN = put("identity", [P, P])
        ONES = put("ones", [P, P])
        CST = put("const_T", [P, 92])
        BC = put("bc_cols", [P, 4, NH, NS])
        COLS = put("gate_cols", [P, NCH, 4, NH])
        SM = put("sample_qkv", [P, 3, NH, NS])
        ST = put("sample_tmp", [P, 10, NH, NS])
        LNT = at("ln_stats", [P, 3, 20], R["sample_tmp"] - 10 * NH * NS * 4)
        US = put("u_last", [P, 4, NBUF + NS])
        NO = put("n_out", [P, 36])
        WSUM = put("win_state", [P, 4, NS])
        SMALL = put("small", [P, 64])
        INV = put("inv_count", [P, 16])
        TAIL = SMALL[:, 49:64]
        o_lay = cur[0]
        E = put("decay", [P, 2, P])
        PT = put("probs", [P, 2, P])
        KW = put("k_weighted", [P, 2, P])
        QI = put("q_inter", [P, 2, P])
        HN = put("h_nat", [P, 2, P])
        VA = put("v_aug", [P, 2, DH + 1])
        CA = put("state_ring", [P, 3, DH + 1])
        WP = put("w_pool_sb", [P, 4, P])
        RBH = put("rows_hi", [P, NT], F32R)
        o_xn = R["rows_hi"] - XROW
        RBL = put("rows_lo", [P, NT], F32R)
        SEL = put("select", [P, 2, NH, P], F32R)
        TA = put("win_a", [P, 8 + NT])
        assert base + cur[0] <= nc.sbuf_usable_end, (base + cur[0], nc.sbuf_usable_end)
        VM = at("v_masked", [P, 2, 4, P], o_lay)
        KVN = at("kv_sample_nat", [P, 2, P], o_lay + 4096)
        XV = at("x1_T", [P, KC, P], o_lay)
        RT = at("relu", [P, 2, BLK], o_lay + 4096)
        SQ = at("relu_sq", [P, 2, BLK], o_lay + 4096 + 2 * BLK * 4)
        assert R["relu_sq"] <= o_xn
        XN = at("x_nat", [P, 2, D], o_xn)
        RS = at("res_nat", [P, 2, D], o_xn + 8192)
        GB = at("ln2_gb", [P, 2, D], o_xn)
        OUT = [at("out0", [P, D], o_xn + 8192), at("out1", [P, D], o_xn + 12288), at("out2", [P, D], o_lay)]
        UN = at("u_nat", [P, 4 * P], o_xn)
        NN = at("n_nat", [P, P], o_xn + 2048)

        bank = [ctx.enter_context(nc.psum_tensor(f"bank{i}", [P, 512], F32)) for i in range(8)]
        B_, S_, T_, D_, N_ = bank[3:8]

        def sem(name):
            return ctx.enter_context(nc.semaphore(name))

        raw_in = [sem("raw_in0"), sem("raw_in1")]
        hi_done, lo_done = sem("hi_done"), sem("lo_done")
        gemm_done, gemm_read = sem("gemm_done"), sem("gemm_read")
        x_in = [sem(f"x_in{t}") for t in range(len(TILES))]
        small_in, bias_in, consts = sem("small_in"), sem("bias_in"), sem("consts")
        xT_ready, x_hi, x_lo = sem("xT_ready"), sem("x_hi_done"), sem("x_lo_done")
        stT_ready, stT_read = sem("stT_ready"), sem("stT_read")
        act_row, dve_row = sem("act_row"), sem("dve_row")
        colT, colT_read = sem("colT"), sem("colT_read")
        pool_step, smp_kept, wsum_ready = sem("pool_step"), sem("smp_kept"), sem("wsum_ready")
        bc_ready, s_ready, kvT_ready = sem("bc_ready"), sem("s_ready"), sem("kvT_ready")
        dC_ready, num_ready = sem("dC_ready"), sem("num_ready")
        E_ready, Em_ready, v_ready = sem("E_ready"), sem("Em_ready"), sem("v_ready")
        hn_ready, P_ready, kw_ready, qi_ready = sem("hn_ready"), sem("P_ready"), sem("kw_ready"), sem("qi_ready")
        C_ready, den_ready, r_ready, y_ready = sem("C_ready"), sem("den_ready"), sem("r_ready"), sem("y_ready")
        ncol_ready, state_out = sem("ncol_ready"), sem("state_out")
        c_in, prod_ready = sem("c_in"), sem("prod_ready")
        smp, smp_y, smp_n = sem("smp_step"), sem("smp_y"), sem("smp_n")
        kvs_T, kvs_read, vm_ready, outer_ready = sem("kvs_T"), sem("kvs_read"), sem("vm_ready"), sem("outer_ready")
        C_new, c_out = sem("C_new"), sem("c_out")
        win_step, pooled, mixed, mixed_read = sem("win_step"), sem("pooled"), sem("mixed"), sem("mixed_read")
        nat_T, nat_read, nat_out, outs = sem("nat_T"), sem("nat_read"), sem("nat_out"), sem("outs")
        cat_hi, cat_lo, heads0_hi = sem("cat_hi"), sem("cat_lo"), sem("heads0_hi")
        xn_in = [sem("xn_in0"), sem("xn_in1")]
        mixT_ready, res_done, ln_stats, ln_sqrt, ln_numbers, ln_norm = (
            sem("mixT_ready"), sem("res_done"), sem("ln_stats"), sem("ln_sqrt"), sem("ln_numbers"), sem("ln_norm"))
        nT_ready, xv_ready, x1_hi, x1_lo, x1_acc = (
            sem("nT_ready"), sem("xv_ready"), sem("x1_hi"), sem("x1_lo"), sem("x1_acc"))
        bf_ready, sq_done, h_hi, h_lo = sem("bf_ready"), sem("sq_done"), sem("h_hi"), sem("h_lo")
        down_done, down_read = sem("down_done"), sem("down_read")
        l2_pool, l2_last = sem("l2_pool"), sem("l2_last")
        gb_in, l2_T, l2_stats, l2_numbers, l2_sqrt, l2_norm, l2_g, l2_b = (
            sem("gb_in"), sem("l2_T"), sem("l2_stats"), sem("l2_numbers"), sem("l2_sqrt"), sem("l2_norm"), sem("l2_g"), sem("l2_b"))
        out_done = [sem(f"out_done{i}") for i in range(3)]

        block = ctx.enter_context(nc.Block())

        def wslot(t, s):
            return t[:, s % 2, :].rearrange("p (k n) -> p k n", k=KC)

        def wslot2(t, s):
            return t[:, s % 2, :].rearrange("p (k n) -> p k n", k=FG // P)

        def gslot(t):
            return t[:, 0, 0:KC * GATE_ROWS].rearrange("p (k n) -> p k n", k=KC)

        def blk(b):
            return slice(BLK * b, BLK * (b + 1))

        w_in_v = a["w_in"][0].rearrange("(k p) n -> p k n", p=P)
        w_out_v = a["w_out"][0].rearrange("(k p) n -> p k n", p=P)
        w1_v = a["w_ff1"][0].rearrange("(k p) n -> p k n", p=P)
        w2_v = a["w_ff2"][0].rearrange("(k p) n -> p k n", p=P)
        G1, B1, B2, PS, BF = 0, 8, 16, 24, 28
        n0T = CST[:, 60:92].rearrange("p (b h) -> p h b", h=NH)
        pr, sa = slice(0, SEQ), slice(SEQ, NT)

        raw_count = [0, 0]
        RAW_AT = []
        for u in range(U_FFN):
            raw_count[u % 2] += 32 if 1 <= u <= 8 else 16
            RAW_AT.append(raw_count[u % 2])

        def outputs_to(u):
            return N_GATE + 6 * u if u < U_OUT else N_PROJ + 2 * (u - U_OUT + 1)

        RAW_AT.append(raw_count[U_FFN % 2] + 16)

        def ffn_raw(i):
            return raw_count[(U_FFN + i) % 2] + 16 * (i // 2 + 1)

        def token_dma(eng, tile, dram_p, dram_s, t, to_sbuf, s):
            t0, n = TILES[t]
            np_ = min(n, SEQ - t0)
            parts = [(tile[0:np_, :], dram_p[0, t0:t0 + np_, :])]
            if np_ < n:
                parts.append((tile[np_:n, :], dram_s[:, 0, :]))
            for sb, dr in parts:
                if to_sbuf:
                    eng.dma_start(sb, dr).then_inc(s, 16)
                else:
                    eng.dma_start(dr, sb).then_inc(s, 16)

        def arrived(t, n_slots):
            return 16 * (t // n_slots + 1 + (t == len(TILES) - 1))

        def pair(p):
            h, j = p // PAIRS, p % PAIRS
            return h, j, slice(2 * P * j, 2 * P * (j + 1))

        def gap_pair(u, i):
            gap = 6 * (u - 3) + i
            return (gap % 3, gap // 3) if gap >= 0 else (None, None)

        UCH = {(9, 0): 3, (9, 1): 2, (10, 0): 1, (10, 1): 0}
        ROW_PAD, ROW_INV, ROW_M, ROW_NEGM, ROW_Z, ROW_A, ROW_W, ROW_LO, ROW_RX = 1, 2, 6, 7, 8, 9, 10, 11, 12
        NPAIR = NH * PAIRS
        LN1_LAST = {1: ((0, 7),), 2: ((1, 6),), 3: ((0, 8),), 4: ((1, 7),), 6: ((1, 8),)}
        L2_BANK = (6, 0, 6, 0, 6, 0, 6, 0, 3)
        LN2_EARLY = {9: 0, 11: 1, 13: 2, 17: 3, 19: 4, 21: 5}

        @block.sync
        def _(sp):
            for t in range(3):
                token_dma(sp, XNAT[0:TILES[t][1], t, :], a["x_prompt"], a["x_sample"], t, True, x_in[t])
            with nc.allow_non_contiguous_dma(reason="eight gate columns"):
                sp.dma_start(wslot(RAW, 0)[:, :, 0:2 * NH], w_in_v[:, :, 2560:2568]).then_inc(raw_in[0], 16)
            for t in range(3, len(TILES)):
                token_dma(sp, XNAT[0:TILES[t][1], t, :], a["x_prompt"], a["x_sample"], t, True, x_in[t])
            for u in range(1, U_OUT):
                kind, j = PROJ[u - 1]
                if u >= 2:
                    sp.wait_ge(lo_done, u - 1)
                slot = wslot(RAW, u)
                if kind == "U":
                    sp.dma_start(slot, w_in_v[:, :, UW * j:UW * (j + 1)]).then_inc(raw_in[u % 2], 16)
                else:
                    for s in range(2):
                        c = 512 + 512 * s + DH * j + (1024 if kind == "B" else 0)
                        sp.dma_start(slot[:, :, P * s:P * (s + 1)], w_in_v[:, :, c:c + P]).then_inc(raw_in[u % 2], 16)
            for u in range(U_OUT, U_FFN):
                j = (u - U_OUT) % (D // UW)
                sp.wait_ge(lo_done, u - 1)
                sp.dma_start(wslot(RAW, u), w_out_v[:, :, UW * j:UW * (j + 1)]).then_inc(raw_in[u % 2], 16)
            with sp.Fori(0, NG) as g:
                for i in range(4):
                    s = U_FFN + i
                    sp.wait_ge(lo_done, g * 4 + (s - 1))
                    if i < 2:
                        src, dst = w1_v[:, :, bass.ds(g * FG + UW * i, UW)], wslot(RAW, s)
                    else:
                        src = w2_v[:, bass.ds(g * (FG // P), FG // P), 512 * (i - 2):512 * (i - 1)]
                        dst = wslot2(RAW, s)
                    sp.dma_start(dst, src).then_inc(raw_in[s % 2], 16)
            for t in range(len(TILES)):
                if t < 8:
                    sp.wait_ge(l2_b, t + 1)
                else:
                    sp.wait_ge(l2_last, 1)
                token_dma(sp, OUT[t % 3][0:TILES[t][1], :], a["y_prompt"], a["y_sample"], t, False, out_done[t % 3])
            for s in range(3):
                sp.wait_ge(out_done[s], arrived(6 + s, 3))

        def norm1(pool, t):
            t0, n = TILES[t]
            q = t % 2
            pool.wait_ge(ln_numbers, 2 * t + 2)
            nc.gpsimd.tensor_scalar(RS[0:n, q, :], RS[0:n, q, :], LNT[0:n, t % 3, 16:17], LNT[0:n, t % 3, 17:18],
                                    ALU.mult, ALU.add).then_inc(ln_norm, 1)

        @block.gpsimd
        def _(pool):
            G = nc.gpsimd
            G.memset(IDN[:, :], 0.0).then_inc(pool_step, 1)
            pool.wait_ge(pool_step, 1)
            G.affine_select(out=IDN[:, :], in_=IDN[:, :], compare_op=ALU.not_equal, fill=1.0, base=0,
                            pattern=[[-1, P]], channel_multiplier=1).then_inc(consts, 1)
            G.memset(ONES[:, :], 1.0).then_inc(consts, 1)
            sel = TA[:, 0:2 * NH * P].rearrange("p (g h m) -> p g h m", g=2, h=NH)
            G.memset(sel, 0.0).then_inc(pool_step, 1)
            pool.wait_ge(pool_step, 2)
            G.affine_select(out=sel, in_=sel, compare_op=ALU.not_equal, fill=1.0, base=0,
                            pattern=[[-32, 2], [-1, NH], [0, P]], channel_multiplier=1).then_inc(pool_step, 1)
            pool.wait_ge(pool_step, 3)
            G.tensor_copy(SEL[:, :, :, :], sel).then_inc(consts, 1)
            G.memset(VA[:, :, DH:DH + 1], 1.0).then_inc(consts, 1)
            r = 0
            for name, n in (("ln1_g", 8), ("ln1_b", 8), ("b_ff2", 8), ("pool_scale", 4), ("b_ff1", 32)):
                pool.dma_start(CN[r:r + n, :], a[name][0].rearrange("(n p) -> n p", p=P)).then_inc(small_in, 16)
                r += n
            pool.dma_start(CN[r:r + 32, :], a["state_n"][0].rearrange("b h d -> (b h) d")).then_inc(small_in, 16)
            pool.dma_start(SPN[0:NS * NBUF, :], a["state_pool"][0].rearrange("b r c -> (b r) c")).then_inc(small_in, 16)
            pool.dma_start(WP[:, :, :], a["w_pool"][0].rearrange("g c d -> c g d")).then_inc(small_in, 16)
            with nc.allow_non_contiguous_dma(reason="a few words"):
                pool.dma_start(SMALL[0:NH, 0:1], a["b_gate"][0:1, 0:NH].rearrange("a h -> h a")).then_inc(bias_in, 16)
                pool.dma_start(SMALL[0:NH, 1:2], a["b_gate"][0:1, NH:2 * NH].rearrange("a h -> h a")).then_inc(bias_in, 16)
                pool.dma_start(SMALL[0:NH, 8:16], a["state_m"][0].rearrange("b h -> h b")).then_inc(bias_in, 16)
            pool.wait_ge(xT_ready, 2 * len(TILES))
            G.memset(RC[:, :], 0.0).then_inc(consts, 1)
            G.memset(TN[0:NH, :], 1.0).then_inc(pool_step, 1)
            pool.wait_ge(pool_step, 4)
            G.memset(TN[0:NH, pr].rearrange("h (c t) -> h c t", t=P)[:, :, 0:1], 0.0).then_inc(consts, 1)
            pool.dma_start(a["pool_s"][0, :, 0:NBUF - 1, :], a["state_pool"][0, :, 1:NBUF, :]).then_inc(outs, 16)

            def keep(h, js):
                for j in js:
                    pool.wait_ge(gemm_read, N_GATE + 12 * h + 3 * j + 3)
                    G.tensor_copy(SM[:, j, h, :], QKV[h % 2][:, j, sa]).then_inc(smp_kept, 1)

            def mask(p):
                pool.wait_ge(E_ready, 2 * (p + 1))
                G.affine_select(out=E[:, :, :], in_=E[:, :, :], compare_op=ALU.is_ge, fill=0.0, base=0,
                                pattern=[[0, 2], [1, P]], channel_multiplier=-1).then_inc(Em_ready, 1)

            def final_state(h):
                pool.wait_ge(C_ready, NCH * (h + 1))
                pool.dma_start(a["C_p"][0, 0, h, :, :], CA[:, NCH % 3, 0:DH]).then_inc(state_out, 16)

            keep(0, (0, 1, 2))
            pool.wait_ge(dve_row, ROW_Z)
            with nc.allow_non_contiguous_dma(reason="a few words"):
                pool.dma_start(a["m_p"][0, 0:1, :].rearrange("a h -> h a"), SMALL[0:NH, 40:41]).then_inc(outs, 16)
                pool.dma_start(a["m_s"][0].rearrange("b h -> h b"), SMALL[0:NH, 41:49]).then_inc(outs, 16)
            for h in range(NH):
                for j in range(PAIRS):
                    mask(PAIRS * h + j)
                    if h < NH - 1 and j == 2:
                        keep(h + 1, (0, 1))
                if h < NH - 1:
                    keep(h + 1, (2,))
                final_state(h)
                if h == NH - 2:
                    pool.wait_ge(num_ready, PAIRS * (NH - 1))
                    for s in range(NH):
                        pool.dma_start(C0[:, s, :, :], a["state_C"][0, :, s, :, :].rearrange("b d e -> d b e"))\
                            .then_inc(c_in, 16)
            pool.wait_ge(nat_read, 1)
            pool.dma_start(a["pool_p"][0, 0, :, :], UN[0:NBUF, :]).then_inc(nat_out, 16)
            pool.dma_start(a["pool_s"][0, :, NBUF - 1, :], UN[NBUF:NBUF + NS, :]).then_inc(nat_out, 16)
            pool.wait_ge(nat_read, 2)
            for h in range(NH):
                pool.dma_start(a["n_s"][0, :, h, :], NN[NS * h:NS * (h + 1), :]).then_inc(nat_out, 16)
            pool.dma_start(a["n_p"][0, 0, :, :], NN[32:36, :]).then_inc(nat_out, 16)
            for h in range(NH):
                pool.wait_ge(C_new, NS * (h + 1))
                pool.dma_start(a["C_s"][0, :, h, :, :].rearrange("b d e -> d b e"), C0[:, h, :, :]).then_inc(c_out, 16)
            pool.wait_ge(nat_out, 16 * 7)
            for t in range(len(TILES)):
                for x in ((0, 1) if t == 0 else (t + 1,)):
                    if x < len(TILES):
                        if x >= 2:
                            pool.wait_ge(res_done, x - 1)
                        token_dma(pool, XN[0:TILES[x][1], x % 2, :], a["x_prompt"], a["x_sample"], x, True, xn_in[x % 2])
                norm1(pool, t)
            pool.wait_ge(res_done, len(TILES))
            for i, name in enumerate(("ln2_g", "ln2_b")):
                pool.dma_start(GB[:, i, :], a[name][0:1, :].to_broadcast([P, D])).then_inc(gb_in, 16)
            pool.wait_ge(gb_in, 32)
            for t, (t0, n) in enumerate(TILES[:8]):
                if t < 6:
                    pool.wait_ge(l2_norm, 2 * t + 2)
                    G.tensor_tensor(OUT[t % 3][0:n, :], OUT[t % 3][0:n, :], GB[0:n, 0, :], ALU.mult).then_inc(l2_pool, 1)
                    pool.wait_ge(l2_pool, t + 1)
                else:
                    pool.wait_ge(l2_g, t - 5)
                G.tensor_tensor(OUT[t % 3][0:n, :], OUT[t % 3][0:n, :], GB[0:n, 1, :], ALU.add).then_inc(l2_b, 1)
            pool.wait_ge(outs, 16 * 3)
            pool.wait_ge(c_out, 16 * NH)
            pool.wait_ge(state_out, 16 * NH)

        @block.scalar
        def _(act):
            A = nc.scalar.activation
            def split_hi(u):
                act.wait_ge(raw_in[u % 2], RAW_AT[u])
                if u >= 2:
                    act.wait_ge(gemm_done, outputs_to(u - 2))
                if u == 0:
                    act.wait_ge(dve_row, ROW_PAD)
                    A(gslot(WH)[:, :, 0:NH], wslot(RAW, 0)[:, :, 0:NH], ACT.Copy)
                    A(gslot(WH)[:, :, 32:32 + NH], wslot(RAW, 0)[:, :, NH:2 * NH], ACT.Copy).then_inc(hi_done, 1)
                else:
                    A(WH[:, u % 2, :], RAW[:, u % 2, :], ACT.Copy).then_inc(hi_done, 1)

            act.wait_ge(consts, 2)
            A(SMALL[:, 3:4], ONES[:, 0:1], ACT.Copy)

            for s in range(2 * len(TILES)):
                t0, n = TILES[s // 2]
                act.wait_ge(xT_ready, s + 1)
                A(XH[:, 4 * (s % 2):4 * (s % 2) + 4, t0:t0 + n],
                  bank[3 + s % 4][:, :].rearrange("p (k n) -> p k n", k=4)[:, :, 0:n], ACT.Copy).then_inc(x_hi, 1)
                if s == 5:
                    split_hi(0)
            split_hi(1)
            act.wait_ge(bias_in, 16 * 3)
            for b in range(NBLK):
                act.wait_ge(gemm_done, b + 1)
                A(TI[0:NH, blk(b)], bank[b][0:NH, 0:BLK], ACT.Identity, bias=SMALL[0:NH, 0:1])
                A(TF[0:NH, blk(b)], bank[b][32:32 + NH, 0:BLK], ACT.Identity, bias=SMALL[0:NH, 1:2]).then_inc(gemm_read, 1)
            act.wait_ge(stT_ready, 1)
            A(CST[:, :], B_[:, 0:92], ACT.Copy).then_inc(stT_read, 1)
            act.wait_ge(stT_ready, 2)
            A(SPT[:, :, :, :].rearrange("p g b r -> p g (b r)"),
              S_[:, :].rearrange("p (g n) -> p g n", g=4)[:, :, 0:NS * NBUF], ACT.Copy).then_inc(stT_read, 1)
            def evac(u, i):
                kind, j = PROJ[u - 1]
                f, b = i // 3, i % 3
                n = N_GATE + 6 * (u - 1) + i
                act.wait_ge(gemm_done, n + 1)
                src = bank[n % 3][:, 0:BLK]
                if kind == "U":
                    A(Y[:, UCH[u, f], blk(b)], src, ACT.Copy).then_inc(gemm_read, 1)
                elif kind == "A":
                    if j >= 2 and i == 0:
                        act.wait_ge(smp_kept, 3 * (j - 1))
                    A(QKV[j % 2][:, f, blk(b)], src, ACT.Copy, scale=(DH ** -0.5 if f else 1.0)).then_inc(gemm_read, 1)
                elif f == 0:
                    A(QKV[j % 2][:, 2, blk(b)], src, ACT.Copy).then_inc(gemm_read, 1)
                else:
                    A(Y[:, 4 + j, blk(b)], src, ACT.Sigmoid).then_inc(gemm_read, 1)

            act.wait_ge(gemm_read, NBLK)
            A(TZ[0:NH, :], TF[0:NH, :], ACT.Abs).then_inc(act_row, 1)
            act.wait_ge(act_row, 1)
            A(TM[0:NH, :], TZ[0:NH, :], ACT.Exp, scale=-1.0).then_inc(act_row, 1)
            act.wait_ge(act_row, 2)
            A(TZ[0:NH, :], TM[0:NH, :], ACT.Ln, bias=1.0).then_inc(act_row, 1)
            evac(1, 0)
            evac(1, 1)
            split_hi(2)
            act.wait_ge(dve_row, ROW_NEGM)
            A(RBH[0:NH, pr], TN[0:NH, pr], ACT.Copy).then_inc(act_row, 1)
            evac(1, 2)
            act.wait_ge(dve_row, ROW_Z)
            act.wait_ge(consts, 5)
            A(RC[32:32 + NH, :], TZ[0:NH, :], ACT.Exp).then_inc(act_row, 1)
            A(RC[96:96 + NH, :], TM[0:NH, :], ACT.Exp, scale=-1.0).then_inc(act_row, 1)
            act.wait_ge(dve_row, ROW_W)
            A(RC[64:64 + NH, :], TBS[0:NH, :], ACT.Exp).then_inc(act_row, 1)
            act.wait_ge(act_row, 5)
            A(RBH[32:32 + NH, :], RC[32:32 + NH, :], ACT.Copy).then_inc(act_row, 1)

            def decay_and_v(p):
                h, j, _ = pair(p)
                act.wait_ge(bc_ready, p + 1)
                if p:
                    act.wait_ge(P_ready, p)
                for i in range(2):
                    A(E[:, i, :], B_[:, P * i:P * (i + 1)], ACT.Exp,
                      bias=COLS[:, 2 * j + i, 0, h:h + 1]).then_inc(E_ready, 1)
                act.wait_ge(kvT_ready, p + 1)
                if p:
                    act.wait_ge(num_ready, p)
                A(VA[:, :, 0:DH], T_[:, 256:512].rearrange("p (i n) -> p i n", i=2), ACT.Copy).then_inc(v_ready, 1)

            def divide(p):
                act.wait_ge(r_ready, p + 1)
                if p:
                    act.wait_ge(s_ready, p + 1)
                for i in range(2):
                    A(HN[:, i, :], N_[:, 129 * i:129 * i + P], ACT.Copy, scale=SMALL[:, 36 + i:37 + i])\
                        .then_inc(hn_ready, 1)

            for u in range(1, U_OUT):
                if u > 1:
                    split_hi(u + 1)
                if u == 3:
                    act.wait_ge(colT_read, 2)
                    act.wait_ge(consts, 4)
                for i in range(3 if u == 1 else 0, 6):
                    evac(u, i)
                    part, p = gap_pair(u, i)
                    if part == 0:
                        decay_and_v(p)
                    elif part == 2:
                        divide(p)
            def cat_hi_part(b, heads):
                ks = slice(4, 8) if heads else slice(0, 4)
                if heads and b == 1:
                    act.wait_ge(y_ready, NPAIR)
                if heads and b == NBLK - 1:
                    act.wait_ge(smp_y, 1)
                if not heads:
                    act.wait_ge(mixed_read, 10 + b)
                A(XH[:, ks, blk(b)], Y[:, ks, blk(b)], ACT.Copy).then_inc(cat_hi, 1)

            for i, g in enumerate((3, 2, 1, 0)):
                for b in range(NBLK):
                    act.wait_ge(mixed, 3 * i + b + 1)
                    A(Y[:, g, blk(b)], bank[b][:, 0:BLK], ACT.Copy, scale=CST[:, PS + g:PS + g + 1]).then_inc(mixed_read, 1)
            cat_hi_part(0, False)
            split_hi(U_OUT + 1)

            def ffn_hi(g, i):
                s = U_FFN + i
                act.wait_ge(raw_in[s % 2], g * 32 + ffn_raw(i))
                if i < 2:
                    act.wait_ge(down_done, g * 24 + (20, 24)[i])
                else:
                    act.wait_ge(gemm_done, g * 12 + (N_OUT + (10, 12)[i - 2]))
                A(WH[:, s % 2, :], RAW[:, s % 2, :], ACT.Copy).then_inc(hi_done, 1)

            def mix_evac(u, f):
                b, j = (u - U_OUT) // 4, (u - U_OUT) % 4
                n = N_PROJ + 2 * (u - U_OUT) + f
                act.wait_ge(gemm_done, n + 1)
                if f == 0 and j == 0:
                    act.wait_ge(cat_lo, 2 * b + 2)
                A(Y[:, 2 * j + f, blk(b)], bank[n % 3][:, 0:BLK], ACT.Copy).then_inc(gemm_read, 1)

            def ln1_sqrt(t):
                n, q = TILES[t][1], t % 3
                act.wait_ge(ln_stats, 3 * t + 3)
                A(LNT[0:n, q, 15:16], LNT[0:n, q, 14:15], ACT.Sqrt).then_inc(ln_sqrt, 1)

            def x1_T(t):
                t0, n = TILES[t]
                act.wait_ge(nT_ready, t + 1)
                if t:
                    act.wait_ge(x1_acc, t)
                else:
                    act.wait_ge(vm_ready, 8)
                    act.wait_ge(outer_ready, 8)
                for f in range(KC):
                    A(XV[:, f, 0:n], (T_, D_)[f // 4][:, P * (f % 4):P * (f % 4) + n], ACT.Identity,
                      scale=CST[:, G1 + f:G1 + f + 1], bias=CST[:, B1 + f:B1 + f + 1]).then_inc(xv_ready, 1)
                act.wait_ge(xv_ready, KC * (t + 1))
                A(XH[:, :, t0:t0 + n], XV[:, :, 0:n], ACT.Copy).then_inc(x1_hi, 1)

            for u in range(U_OUT, U_FFN):
                b, j = (u - U_OUT) // 4, (u - U_OUT) % 4
                mix_evac(u, 0)
                if u == U_OUT:
                    act.wait_ge(nat_T, 1)
                    A(UN[0:NBUF + NS, :], B_[0:NBUF + NS, :], ACT.Copy).then_inc(nat_read, 1)
                    act.wait_ge(kvs_T, 1)
                    A(KVN[0:32, :, :], T_[0:32, 0:256].rearrange("p (i n) -> p i n", i=2), ACT.Copy).then_inc(kvs_read, 1)
                    act.wait_ge(nat_T, 2)
                    A(NN[0:36, :], D_[0:36, 0:P], ACT.Copy).then_inc(nat_read, 1)
                if b and j < 3:
                    ln1_sqrt(3 * (b - 1) + j)
                mix_evac(u, 1)
                if u < U_FFN - 1:
                    split_hi(u + 2)
                else:
                    ffn_hi(0, 1)
                if b == 0:
                    cat_hi_part(1 + j // 2, j % 2 == 0)
                elif j >= 1:
                    x1_T(3 * (b - 1) + j - 1)

            def hidden(g, i):
                n, c = N_OUT + i, i % 4
                act.wait_ge(gemm_done, g * 12 + (n + 1))
                act.wait_ge(h_hi, g * 12 + (i + 1))
                A(RT[:, i % 2, :], bank[n % 3][:, 0:BLK], ACT.Relu,
                  bias=SMALL[:, 4 + c:5 + c]).then_inc(gemm_read, 1)
                act.wait_ge(gemm_read, g * 12 + (n + 1))
                act.wait_ge(h_lo, g * 12 + (i + 1))
                A(SQ[:, i % 2, :], RT[:, i % 2, :], ACT.Square).then_inc(sq_done, 1)

            def mlp_step(g, between=None, last=False):
                A(SMALL[:, 4:8], CST[:, bass.ds(g * 4 + BF, 4)], ACT.Copy).then_inc(bf_ready, 1)
                if between is None:
                    ffn_hi(g, 1)
                act.wait_ge(bf_ready, g + 1)
                for i in range(12):
                    if i == 10:
                        ffn_hi(g, 2)
                    hidden(g, i)
                    if between:
                        between(i)
                ffn_hi(g, 3)
                if not last:
                    ffn_hi(g + 1, 0)

            def last_ln1(i):
                for kind, t in LN1_LAST.get(i, ()):
                    (ln1_sqrt, x1_T)[kind](t)

            act.wait_ge(state_out, 16 * NH)
            ln1_sqrt(6)
            mlp_step(0, last_ln1)
            with act.Fori(1, NG - 1) as g:
                mlp_step(g)
            mlp_step(NG - 1, last=True)

            def l2_root(t):
                n, q = TILES[t][1], t % 3
                act.wait_ge(l2_stats, 3 * t + 3)
                A(LNT[0:n, q, 15:16], LNT[0:n, q, 14:15], ACT.Sqrt).then_inc(l2_sqrt, 1)

            def l2_normed(t):
                n, q = TILES[t][1], t % 3
                act.wait_ge(l2_numbers, 2 * t + 2)
                if t >= 3:
                    act.wait_ge(out_done[t % 3], 16 * (t // 3))
                for half in range(2):
                    A(OUT[t % 3][0:n, 512 * half:512 * (half + 1)], bank[L2_BANK[t] + half][0:n, :], ACT.Identity,
                      bias=LNT[0:n, q, 17:18], scale=LNT[0:n, q, 16:17]).then_inc(l2_norm, 1)

            for t in range(6):
                l2_root(t)
                l2_normed(t)
            l2_root(6)
            l2_root(7)
            l2_normed(6)
            l2_root(8)
            l2_normed(7)
            l2_normed(8)

        @block.vector
        def _(dve):
            V = nc.vector
            stt = V.scalar_tensor_tensor

            def split_lo(u):
                dve.wait_ge(hi_done, u + 1)
                if u == 0:
                    raw, hi, lo = wslot(RAW, 0), gslot(WH).bitcast(F32), gslot(WL)
                    V.tensor_tensor(lo[:, :, 0:NH], raw[:, :, 0:NH], hi[:, :, 0:NH], ALU.subtract)
                    V.tensor_tensor(lo[:, :, 32:32 + NH], raw[:, :, NH:2 * NH], hi[:, :, 32:32 + NH],
                                    ALU.subtract).then_inc(lo_done, 1)
                else:
                    V.tensor_tensor(WL[:, u % 2, :], RAW[:, u % 2, :], WH[:, u % 2, :].bitcast(F32),
                                    ALU.subtract).then_inc(lo_done, 1)

            row_n = [0]

            def row(ins, value=None):
                row_n[0] += 1
                ins.then_inc(dve_row, 1)
                assert value in (None, row_n[0]), (value, row_n[0])

            def after_rows():
                dve.wait_ge(dve_row, row_n[0])

            V.memset(WL[:, 0, 0:KC * GATE_ROWS].bitcast(F32), 0.0)
            row(V.memset(WH[:, 0, 0:KC * GATE_ROWS].bitcast(F32), 0.0), ROW_PAD)
            after_rows()
            for j in range(NBUF - 1):
                V.memset(INV[:, j:j + 1], 1.0 / (j + 1))
            V.memset(INV[:, NBUF - 1:NBUF], 1.0 / NBUF)
            V.memset(RBH[:, :].bitcast(F32), 0.0)
            row(V.memset(RBL[:, :].bitcast(F32), 0.0), ROW_INV)
            for s in range(2 * len(TILES)):
                t0, n = TILES[s // 2]
                ks = slice(4 * (s % 2), 4 * (s % 2) + 4)
                dve.wait_ge(x_hi, s + 1)
                V.tensor_tensor(XL[:, ks, t0:t0 + n],
                                bank[3 + s % 4][:, :].rearrange("p (k n) -> p k n", k=4)[:, :, 0:n],
                                XH[:, ks, t0:t0 + n].bitcast(F32), ALU.subtract).then_inc(x_lo, 1)
                if s == 5:
                    split_lo(0)
            split_lo(1)
            dve.wait_ge(stT_read, 2)
            for g, w in enumerate(WINDOWS):
                V.tensor_reduce(WSUM[:, g, :], SPT[:, g, :, NBUF - (w - 1):NBUF], AX.X, ALU.add).then_inc(wsum_ready, 1)

            def chunks(t):
                return t[0:NH, pr].rearrange("h (c t) -> h c t", t=P)

            dve.wait_ge(act_row, 3)
            row(stt(TF[0:NH, :], TF[0:NH, :], 0.0, TZ[0:NH, :], ALU.min, ALU.subtract))
            dve.wait_ge(consts, 6)
            dve.wait_ge(bias_in, 16 * 3)
            after_rows()
            V.tensor_tensor_scan(TBS[0:NH, pr], TN[0:NH, pr], TF[0:NH, pr], 0.0, ALU.mult, ALU.add)
            V.tensor_tensor_scan(TM[0:NH, pr], TF[0:NH, pr], TI[0:NH, pr], 0.0, ALU.add, ALU.max)
            row(V.tensor_tensor(SMALL[0:NH, 16:24], TF[0:NH, sa], SMALL[0:NH, 8:16], ALU.add))
            after_rows()
            row(V.tensor_tensor(TM[0:NH, sa], SMALL[0:NH, 16:24], TI[0:NH, sa], ALU.max))
            after_rows()
            V.tensor_copy(SMALL[0:NH, 40:49], TM[0:NH, SEQ - 1:NT])
            V.memset(SMALL[0:NH, 24:25], 0.0)
            row(V.tensor_copy(SMALL[0:NH, 25:32], chunks(TM)[:, 0:NCH - 1, P - 1]), ROW_M)
            row(V.tensor_tensor(TN[0:NH, pr], TBS[0:NH, pr], TM[0:NH, pr], ALU.subtract), ROW_NEGM)
            after_rows()
            V.tensor_tensor(chunks(TZ), chunks(TN), SMALL[0:NH, 24:32].rearrange("h (c o) -> h c o", o=1)
                            .to_broadcast([NH, NCH, P]), ALU.add)
            row(V.tensor_tensor(TZ[0:NH, sa], SMALL[0:NH, 16:24], TM[0:NH, sa], ALU.subtract), ROW_Z)
            row(V.tensor_tensor(RC[0:NH, pr], TI[0:NH, pr], TBS[0:NH, pr], ALU.subtract), ROW_A)
            after_rows()
            V.tensor_tensor(chunks(TBS), chunks(RC), chunks(TN)[:, :, P - 1:P].to_broadcast([NH, NCH, P]), ALU.add)
            row(V.tensor_tensor(TBS[0:NH, sa], TI[0:NH, sa], TM[0:NH, sa], ALU.subtract), ROW_W)
            split_lo(2)
            dve.wait_ge(act_row, 8)
            V.tensor_tensor(RBL[0:NH, pr], TN[0:NH, pr], RBH[0:NH, pr].bitcast(F32), ALU.subtract)
            row(V.tensor_tensor(RBL[32:32 + NH, :], RC[32:32 + NH, :], RBH[32:32 + NH, :].bitcast(F32),
                                ALU.subtract), ROW_LO)
            last_of_chunk = RC[:, pr].rearrange("p (o c t) -> p o c t", o=1, t=P)[:, :, :, P - 1]
            of_samples = RC[:, sa].rearrange("p (o c) -> p o c", o=1)
            for i, (g, src) in enumerate(((1, last_of_chunk), (1, of_samples), (2, of_samples), (3, of_samples))):
                onehot = IDN[:, 32 * g:32 * g + NH].rearrange("p (h o) -> p h o", o=1).to_broadcast([P, NH, NS])
                ins = V.tensor_tensor(ST[:, i, :, :], src.to_broadcast([P, NH, NS]), onehot, ALU.mult)
            row(ins, ROW_RX)

            def gate_columns():
                for i in range(2):
                    dve.wait_ge(colT, i + 1)
                    V.tensor_copy(COLS[:, 4 * i:4 * i + 4, :, :],
                                  (T_, D_)[i][:, :].rearrange("p (c g r) -> p c g r", c=4, g=4)[:, :, :, 0:NH])\
                        .then_inc(colT_read, 1)
                dve.wait_ge(colT, 3)
                V.tensor_copy(BC[:, :, :, :].rearrange("p k h b -> p (k h b)"), N_[:, 0:P]).then_inc(colT_read, 1)

            def gate_h(p):
                h, j, cs = pair(p)
                dve.wait_ge(s_ready, p + 2)
                V.tensor_tensor(Y[:, 4 + h, cs], S_[:, 256:512], Y[:, 4 + h, cs], ALU.mult).then_inc(y_ready, 1)

            def att1(p):
                h, j, cs = pair(p)
                dve.wait_ge(E_ready, 2 * (p + 1))
                if p:
                    dve.wait_ge(num_ready, p)
                V.tensor_tensor(QI[:, :, :].rearrange("p i n -> p (i n)"), QKV[h % 2][:, 0, cs], B_[:, 256:512],
                                ALU.mult).then_inc(qi_ready, 1)
                dve.wait_ge(v_ready, p + 1)
                V.tensor_tensor(KW[:, :, :], T_[:, 0:256].rearrange("p (i n) -> p i n", i=2),
                                COLS[:, 2 * j:2 * j + 2, 2, h:h + 1].to_broadcast([P, 2, P]), ALU.mult).then_inc(kw_ready, 1)
                dve.wait_ge(s_ready, p + 1)
                dve.wait_ge(Em_ready, p + 1)
                V.tensor_tensor(PT[:, :, :].rearrange("p i n -> p (i n)"), S_[:, 0:256],
                                E[:, :, :].rearrange("p i n -> p (i n)"), ALU.mult).then_inc(P_ready, 1)
                if p:
                    gate_h(p - 1)

            def att2(p):
                h, j, _ = pair(p)
                dve.wait_ge(dC_ready, p + 1)
                for i in range(2):
                    c = 2 * j + i
                    new, old, d = CA[:, (c + 1) % 3, :], CA[:, c % 3, :], D_[:, 129 * i:129 * (i + 1)]
                    if c == 0:
                        V.tensor_copy(new, d).then_inc(C_ready, 1)
                    else:
                        if c == 1 and h:
                            dve.wait_ge(state_out, 16 * h)
                        dve.wait_ge(C_ready, NCH * h + c)
                        stt(new, old, BC[:, 0, h, c:c + 1], d, ALU.mult, ALU.add).then_inc(C_ready, 1)

            def att3(p):
                h, j, _ = pair(p)
                dve.wait_ge(num_ready, p + 1)
                den = N_[:, 0:258].rearrange("p (i n) -> p i n", i=2)[:, :, DH]
                V.tensor_tensor(SMALL[:, 32:34], den, COLS[:, 2 * j:2 * j + 2, 3, h], ALU.max).then_inc(den_ready, 1)
                dve.wait_ge(den_ready, 2 * p + 1)
                stt(SMALL[:, 34:36], den, -1.0, SMALL[:, 32:34], ALU.mult, ALU.max).then_inc(den_ready, 1)
                dve.wait_ge(den_ready, 2 * p + 2)
                if p:
                    dve.wait_ge(hn_ready, 2 * p)
                if p >= NPAIR - NH:
                    V.tensor_copy(ST[:, 7, p - (NPAIR - NH), :], N_[:, 264:264 + NS])
                if p == NPAIR - NH:
                    V.tensor_copy(ST[:, 5:7, :, :].rearrange("p a h b -> p (a h b)"), N_[:, 300:364])
                V.reciprocal(SMALL[:, 36:38], SMALL[:, 34:36]).then_inc(r_ready, 1)
                if j == PAIRS - 1:
                    dve.wait_ge(C_ready, NCH * (h + 1))
                    V.tensor_copy(NO[:, 32 + h:33 + h], CA[:, NCH % 3, DH:DH + 1]).then_inc(ncol_ready, 1)

            win_n = [0]

            def win(ins):
                win_n[0] += 1
                ins.then_inc(win_step, 1)
                dve.wait_ge(win_step, win_n[0])

            def window(g, n_out):
                w = WINDOWS[g]
                u = Y[:, g, :]
                dve.wait_ge(gemm_read, n_out)
                V.tensor_copy(US[:, g, :], u[:, SEQ - NBUF:NT])
                V.tensor_copy(TA[:, 8:9], u[:, 0:1])
                V.tensor_tensor(ST[:, 9, 0, :], WSUM[:, g, :], u[:, sa], ALU.add)
                win(V.tensor_tensor(TA[:, 9:8 + SEQ], u[:, 1:SEQ], u[:, 0:SEQ - 1], ALU.add))
                src, dst, d = TA, TB, 2
                while d < w:
                    win(V.tensor_tensor(dst[:, 8:8 + SEQ], src[:, 8:8 + SEQ], src[:, 8 - d:8 - d + SEQ], ALU.add))
                    src, dst, d = dst, src, 2 * d
                win(V.tensor_tensor(TAIL[:, 0:w - 1], src[:, 8:8 + w - 1], INV[:, 0:w - 1], ALU.mult))
                win(V.tensor_tensor(TAIL[:, 0:w - 1], TAIL[:, 0:w - 1], u[:, 0:w - 1], ALU.subtract))
                V.tensor_copy(u[:, 0:w - 1], TAIL[:, 0:w - 1])
                stt(u[:, w - 1:SEQ], src[:, 8 + w - 1:8 + SEQ], 1.0 / w, u[:, w - 1:SEQ], ALU.mult, ALU.subtract)
                stt(u[:, sa], ST[:, 9, 0, :], 1.0 / w, u[:, sa], ALU.mult, ALU.subtract).then_inc(pooled, 1)

            smp_c = [0]

            def step(ins):
                smp_c[0] += 1
                ins.then_inc(smp, 1)
                dve.wait_ge(smp, smp_c[0])

            q_s, k_s, v_s = SM[:, 0, :, :], SM[:, 1, :, :], SM[:, 2, :, :]
            iw_s, dw_s, em_s = BC[:, 1, :, :], BC[:, 2, :, :], BC[:, 3, :, :]
            for u in range(1, U_OUT):
                if u > 1:
                    split_lo(u + 1)
                if u == 2:
                    gate_columns()
                    dve.wait_ge(colT_read, 3)
                    dve.wait_ge(wsum_ready, 4)
                if u == 9:
                    dve.wait_ge(smp_kept, 3 * NH)
                    V.tensor_tensor(ST[:, 0, :, :], q_s, k_s, ALU.mult)
                    step(V.tensor_tensor(ST[:, 2, :, :], q_s, iw_s, ALU.mult))
                    V.tensor_tensor(ST[:, 1, :, :], n0T, ST[:, 2, :, :], ALU.mult).then_inc(prod_ready, 1)
                    V.memset(TA[:, 0:8], 0.0)
                    win(V.memset(TB[:, 0:8], 0.0))
                for i in range(6):
                    part, p = gap_pair(u, i)
                    if part is not None:
                        (att1, att2, att3)[part](p)
                    if u >= 9 and i in (3, 5):
                        window(UCH[u, i // 4], N_GATE + 6 * (u - 1) + (3 if i == 3 else 6))
            gate_h(NPAIR - 1)

            def cat_lo_part(b, heads):
                ks = slice(4, 8) if heads else slice(0, 4)
                if heads and b == 0:
                    dve.wait_ge(y_ready, NPAIR)
                    V.tensor_copy(XH[:, ks, blk(b)], Y[:, ks, blk(b)]).then_inc(heads0_hi, 1)
                    dve.wait_ge(heads0_hi, 1)
                else:
                    dve.wait_ge(cat_hi, 2 * b + (0 if heads else 1))
                V.tensor_tensor(XL[:, ks, blk(b)], Y[:, ks, blk(b)], XH[:, ks, blk(b)].bitcast(F32),
                                ALU.subtract).then_inc(cat_lo, 1)

            s_, nq, num = ST[:, 5, :, :], ST[:, 6, :, :], ST[:, 7, :, :]
            step(V.tensor_tensor(s_, s_, dw_s, ALU.mult))
            V.tensor_tensor(ST[:, 3, :, :], s_, v_s, ALU.mult)
            step(V.tensor_tensor(nq, nq, s_, ALU.add))
            V.tensor_tensor(num, num, ST[:, 3, :, :], ALU.add)
            step(V.tensor_tensor(ST[:, 4, :, :], nq, em_s, ALU.max))
            cat_lo_part(0, True)
            step(stt(nq, nq, -1.0, ST[:, 4, :, :], ALU.mult, ALU.max))
            step(V.reciprocal(ST[:, 4, :, :], nq))
            step(V.tensor_tensor(num, num, ST[:, 4, :, :], ALU.mult))
            V.tensor_tensor(Y[:, 4:8, sa], Y[:, 4:8, sa], num, ALU.mult).then_inc(smp_y, 1)
            V.tensor_tensor(ST[:, 0, :, :], k_s, dw_s, ALU.mult)
            V.tensor_tensor(ST[:, 8, :, :], v_s, dw_s, ALU.mult).then_inc(smp_n, 1)
            NO_s = NO[:, 0:32].rearrange("p (h b) -> p h b", h=NH)
            step(V.tensor_tensor(NO_s, n0T, iw_s, ALU.mult))
            V.tensor_tensor(NO_s, NO_s, ST[:, 0, :, :], ALU.add).then_inc(smp_n, 1)
            cat_lo_part(0, False)
            split_lo(U_OUT + 1)

            def vmask(i):
                dve.wait_ge(kvs_read, 1)
                if i >= 2:
                    dve.wait_ge(outer_ready, i - 1)
                V.tensor_tensor(VM[0:32, i % 2, :, :], KVN[0:32, 1:2, :].to_broadcast([32, 4, P]),
                                IDN[0:32, 4 * i:4 * i + 4].rearrange("p (a o) -> p a o", o=1).to_broadcast([32, 4, P]),
                                ALU.mult).then_inc(vm_ready, 1)

            def new_C(i):
                dve.wait_ge(outer_ready, i + 1)
                for x in range(4):
                    h, s = (4 * i + x) // NS, (4 * i + x) % NS
                    stt(C0[:, h, s, :], C0[:, h, s, :], BC[:, 1, h, s:s + 1], (B_, N_)[i % 2][:, P * x:P * (x + 1)],
                        ALU.mult, ALU.add).then_inc(C_new, 1)

            def variance(x0, x1, t, stats):
                L = LNT[0:TILES[t][1], t % 3, :]
                V.bn_stats(L[:, 0:6], x0)
                V.bn_stats(L[:, 6:12], x1).then_inc(stats, 1)
                dve.wait_ge(stats, 3 * t + 1)
                V.bn_aggr(L[:, 12:14], L[:, 0:12]).then_inc(stats, 1)
                dve.wait_ge(stats, 3 * t + 2)
                V.tensor_scalar(L[:, 14:15], L[:, 13:14], EPS, None, ALU.add).then_inc(stats, 1)

            def scale_and_shift(t, sqrt_done, numbers):
                L = LNT[0:TILES[t][1], t % 3, :]
                dve.wait_ge(sqrt_done, t + 1)
                V.reciprocal(L[:, 16:17], L[:, 15:16]).then_inc(numbers, 1)
                dve.wait_ge(numbers, 2 * t + 1)
                stt(L[:, 17:18], L[:, 12:13], -1.0, L[:, 16:17], ALU.mult, ALU.mult).then_inc(numbers, 1)

            def ln1_a(t):
                n, q = TILES[t][1], t % 2
                dve.wait_ge(xn_in[q], arrived(t, 2))
                dve.wait_ge(mixT_ready, t + 1)
                if t >= 2:
                    dve.wait_ge(nT_ready, t - 1)
                for half in range(2):
                    cs = slice(512 * half, 512 * (half + 1))
                    last = stt(RS[0:n, q, cs], XN[0:n, q, cs], ALPHA, (B_, S_)[half][0:n, :], ALU.mult, ALU.add)
                last.then_inc(res_done, 1)
                dve.wait_ge(res_done, t + 1)
                variance(RS[0:n, q, 0:512], RS[0:n, q, 512:1024], t, ln_stats)
                scale_and_shift(t, ln_sqrt, ln_numbers)

            def ln1_b(t):
                t0, n = TILES[t]
                dve.wait_ge(x1_hi, t + 1)
                V.tensor_tensor(XL[:, :, t0:t0 + n], XV[:, :, 0:n], XH[:, :, t0:t0 + n].bitcast(F32),
                                ALU.subtract).then_inc(x1_lo, 1)
                stt(Y[:, :, t0:t0 + n], XV[:, :, 0:n], ALPHA, CST[:, B2:B2 + 8].rearrange("p (k o) -> p k o", o=1)
                    .to_broadcast([P, KC, n]), ALU.mult, ALU.add).then_inc(x1_acc, 1)

            def ffn_lo(g, i):
                s = U_FFN + i
                dve.wait_ge(hi_done, g * 4 + (s + 1))
                V.tensor_tensor(WL[:, s % 2, :], RAW[:, s % 2, :], WH[:, s % 2, :].bitcast(F32),
                                ALU.subtract).then_inc(lo_done, 1)

            for u in range(U_OUT, U_FFN):
                b, j = (u - U_OUT) // 4, (u - U_OUT) % 4
                if u == U_OUT:
                    vmask(0)
                if b == 0:
                    vmask(2 * j + 1)
                    new_C(2 * j)
                    split_lo(u + 2)
                    if j < 3:
                        vmask(2 * j + 2)
                    new_C(2 * j + 1)
                    cat_lo_part(1 + j // 2, j % 2 == 0)
                else:
                    t = 3 * (b - 1) + j
                    if j < 3:
                        ln1_a(t)
                    if j >= 2 or b == 2 and j == 0:
                        ln1_b(t - 2 if j else t - 1)
                    if u < U_FFN - 1:
                        split_lo(u + 2)
                    else:
                        ffn_lo(0, 1)
            dve.sem_inc(h_hi, 2)
            dve.sem_inc(h_lo, 2)
            dve.sem_inc(down_read, 3)
            dve.wait_ge(c_out, 16 * NH)

            def hidden(g, i):
                c, b = i % 4, i // 4
                dve.wait_ge(sq_done, g * 12 + (i + 1))
                V.tensor_tensor(HH[:, c, blk(b)], RT[:, i % 2, :], RT[:, i % 2, :], ALU.mult).then_inc(h_hi, 1)
                dve.wait_ge(h_hi, g * 12 + (i + 3))
                V.tensor_tensor(HL[:, c, blk(b)], SQ[:, i % 2, :], HH[:, c, blk(b)].bitcast(F32),
                                ALU.subtract).then_inc(h_lo, 1)

            def add_down(g, m):
                o, b = m % 8, m // 8
                dve.wait_ge(down_done, g * 24 + (24 + m + 1))
                V.tensor_tensor(Y[:, o, blk(b)], Y[:, o, blk(b)], bank[3 + m % 3][:, 0:BLK], ALU.add).then_inc(down_read, 1)

            def mlp_step(g, between=None, after=None):
                if between is None:
                    ffn_lo(g, 1)
                for i in range(12):
                    if i == 10:
                        ffn_lo(g, 2)
                    hidden(g, i)
                    if between:
                        between(i)
                ffn_lo(g, 3)
                for m in range(24):
                    if m == 20 and after is None:
                        ffn_lo(g + 1, 0)
                    add_down(g, m)
                    if after:
                        after(m)

            def last_ln1(i):
                for kind, t in LN1_LAST.get(i, ()):
                    (ln1_a, ln1_b)[kind](t)

            def ln2_variance(t):
                n = TILES[t][1]
                dve.wait_ge(l2_T, t + 1)
                if t >= 3:
                    dve.wait_ge(l2_norm, 2 * (t - 2))
                variance(bank[L2_BANK[t]][0:n, :], bank[L2_BANK[t] + 1][0:n, :], t, l2_stats)

            def ln2_gain(t):
                n = TILES[t][1]
                dve.wait_ge(l2_norm, 2 * t + 2)
                V.tensor_tensor(OUT[t % 3][0:n, :], OUT[t % 3][0:n, :], GB[0:n, 0, :], ALU.mult).then_inc(l2_g, 1)

            def early_ln2(m):
                if m in LN2_EARLY:
                    ln2_variance(LN2_EARLY[m])
                    scale_and_shift(LN2_EARLY[m], l2_sqrt, l2_numbers)

            ln1_a(6)
            ln1_b(5)
            mlp_step(0, last_ln1)
            with dve.Fori(1, NG - 1) as g:
                mlp_step(g)
            mlp_step(NG - 1, after=early_ln2)
            dve.wait_ge(gb_in, 32)
            ln2_variance(6)
            ln2_variance(7)
            scale_and_shift(6, l2_sqrt, l2_numbers)
            ln2_variance(8)
            scale_and_shift(7, l2_sqrt, l2_numbers)
            ln2_gain(6)
            scale_and_shift(8, l2_sqrt, l2_numbers)
            ln2_gain(7)
            ln2_gain(8)
            n = TILES[8][1]
            dve.wait_ge(l2_g, 3)
            V.tensor_tensor(OUT[2][0:n, :], OUT[2][0:n, :], GB[0:n, 1, :], ALU.add).then_inc(l2_last, 1)

        @block.tensor
        def _(pe):
            def mm(out, lhsT, rhs, start=True, stop=True):
                return nc.tensor.matmul(out, lhsT, rhs, start=start, stop=stop, skip_group_check=True)

            def tr(out, in_):
                n = in_.shape[0]
                return nc.tensor.transpose(out, in_, IDN[0:n, 0:n])

            def split_product(out, w_hi, w_lo, x_hi_, x_lo_, ks, before=None):
                for i, k in enumerate(ks):
                    if before:
                        before(k)
                    mm(out, w_hi(k), x_hi_(k), i == 0, False)
                    mm(out, w_hi(k), x_lo_(k), False, False)
                    last = mm(out, w_lo(k), x_hi_(k), False, i == len(ks) - 1)
                return last

            def x_block(b):
                for s in range(6 * b, 6 * b + 6):
                    t, half = s // 2, s % 2
                    n = TILES[t][1]
                    if half == 0:
                        pe.wait_ge(x_in[t], 32 if t == len(TILES) - 1 else 16)
                    if s >= 4:
                        pe.wait_ge(x_lo, s - 3)
                    for k in range(4):
                        last = tr(bank[3 + s % 4][:, P * k:P * k + n],
                                  XNAT[0:n, t, P * (4 * half + k):P * (4 * half + k + 1)])
                    last.then_inc(xT_ready, 1)

            def gates(b):
                pe.wait_ge(x_lo, 6 * b + 6)
                split_product(bank[b][0:GATE_ROWS, 0:BLK], lambda k: gslot(WH)[:, k, :], lambda k: gslot(WL)[:, k, :],
                              lambda k: XH[:, k, blk(b)], lambda k: XL[:, k, blk(b)], range(KC)).then_inc(gemm_done, 1)

            pe.wait_ge(consts, 1)
            x_block(0)
            x_block(1)
            pe.wait_ge(lo_done, 1)
            gates(0)
            x_block(2)
            gates(1)
            gates(2)
            pe.wait_ge(small_in, 16 * 8)
            pe.wait_ge(x_lo, 2 * len(TILES))
            tr(B_[:, 0:92], CN[0:92, :]).then_inc(stT_ready, 1)
            for g in range(4):
                last = tr(S_[:, P * g:P * g + NS * NBUF], SPN[0:NS * NBUF, P * g:P * (g + 1)])
            last.then_inc(stT_ready, 1)

            def unit_product(u, f, b, n, ks=range(KC), before=None):
                pe.wait_ge(gemm_read, n - 2)
                cs = slice(P * f, P * (f + 1))
                return split_product(bank[n % 3][:, 0:BLK], lambda k: wslot(WH, u)[:, k, cs], lambda k: wslot(WL, u)[:, k, cs],
                                     lambda k: XH[:, k, blk(b)], lambda k: XL[:, k, blk(b)], ks, before)

            def att1(p):
                if p:
                    pe.wait_ge(hn_ready, 2 * p)
                    pe.wait_ge(P_ready, p)
                    if p >= 2:
                        pe.wait_ge(y_ready, p - 1)
                    for i in range(2):
                        last = tr(S_[:, 256 + P * i:256 + P * (i + 1)], HN[:, i, :])
                    if p == NPAIR:
                        last.then_inc(s_ready, 1)
                        return
                    pe.wait_ge(qi_ready, p)
                    pe.wait_ge(kw_ready, p)
                h, j, cs = pair(p)
                kT, qT, vT = QKV[h % 2][:, 1, :], QKV[h % 2][:, 0, :], QKV[h % 2][:, 2, :]
                for g in range(2):
                    mm(B_[:, 256 * g:256 * (g + 1)], SEL[:, g, h, :], RBH[:, cs], True, False)
                    last = mm(B_[:, 256 * g:256 * (g + 1)], SEL[:, g, h, :], RBL[:, cs], False, True)
                last.then_inc(bc_ready, 1)
                for i in range(2):
                    c = slice(P * (2 * j + i), P * (2 * j + i + 1))
                    last = mm(S_[:, P * i:P * (i + 1)], kT[:, c], qT[:, c])
                last.then_inc(s_ready, 1)
                for x, src in enumerate((kT, vT)):
                    for i in range(2):
                        c = slice(P * (2 * j + i), P * (2 * j + i + 1))
                        last = tr(T_[:, 256 * x + P * i:256 * x + P * (i + 1)], src[:, c])
                last.then_inc(kvT_ready, 1)

            def att2(p):
                pe.wait_ge(kw_ready, p + 1)
                if p:
                    pe.wait_ge(C_ready, 2 * p)
                for i in range(2):
                    last = mm(D_[:, 129 * i:129 * (i + 1)], KW[:, i, :], VA[:, i, :])
                last.then_inc(dC_ready, 1)

            def att3(p):
                h, j, _ = pair(p)
                pe.wait_ge(P_ready, p + 1)
                pe.wait_ge(qi_ready, p + 1)
                pe.wait_ge(C_ready, 2 * p + 1)
                if p:
                    pe.wait_ge(hn_ready, 2 * p)
                for i in range(2):
                    c = 2 * j + i
                    out = N_[:, 129 * i:129 * (i + 1)]
                    last = mm(out, PT[:, i, :], VA[:, i, :], True, c == 0)
                    if c:
                        last = mm(out, QI[:, i, :], CA[:, c % 3, :], False, True)
                if p >= NPAIR - NH:
                    s = p - (NPAIR - NH)
                    if s == 0:
                        pe.wait_ge(c_in, 16 * NH)
                        pe.wait_ge(prod_ready, 1)
                        mm(N_[:, 300:364], ONES[:, :], ST[:, 0:2, :, :].rearrange("p a h b -> p (a h b)"))
                    for b in range(NS):
                        last = mm(N_[:, 264 + b:265 + b], C0[:, s, b, :], ST[:, 2, s, b:b + 1])
                last.then_inc(num_ready, 1)

            for u in range(1, U_OUT):
                pe.wait_ge(lo_done, u + 1)
                if u == 3:
                    pe.wait_ge(colT_read, 3)
                    pe.wait_ge(consts, 4)
                for i in range(6):
                    n = N_GATE + 6 * (u - 1) + i
                    f = UCH[u, i // 3] % 2 if u >= 9 else i // 3
                    unit_product(u, f, i % 3, n).then_inc(gemm_done, 1)
                    if u == 2 and i == 1:
                        pe.wait_ge(dve_row, ROW_RX)
                        pe.wait_ge(stT_read, 2)
                        for x in range(2):
                            for c in range(4):
                                last = tr((T_, D_)[x][:, P * c:P * (c + 1)], RC[:, P * (4 * x + c):P * (4 * x + c + 1)])
                            last.then_inc(colT, 1)
                        mm(N_[:, 0:P], ONES[:, :], ST[:, 0:4, :, :].rearrange("p a h b -> p (a h b)")).then_inc(colT, 1)
                    part, p = gap_pair(u, i)
                    if part is not None:
                        (att1, att2, att3)[part](p)

            for i, g in enumerate((3, 2, 1, 0)):
                pe.wait_ge(pooled, i + 1)
                for b in range(NBLK):
                    if i == 0:
                        pe.wait_ge(gemm_read, N_PROJ - 2 + b)
                    else:
                        pe.wait_ge(mixed_read, 3 * (i - 1) + b + 1)
                    mm(bank[b][:, 0:BLK], WP[:, g, :], Y[:, g, blk(b)]).then_inc(mixed, 1)
                if i == 0:
                    att1(NPAIR)

            def outer(i):
                pe.wait_ge(vm_ready, i + 1)
                if i >= 2:
                    pe.wait_ge(C_new, 4 * (i - 1))
                mm((B_, N_)[i % 2][:, :], KVN[0:32, 0, :],
                   VM[0:32, i % 2, :, :].rearrange("p a n -> p (a n)")).then_inc(outer_ready, 1)

            def mix_T(t):
                t0, n = TILES[t]
                pe.wait_ge(gemm_read, N_PROJ + KC * (t // 3 + 1))
                if t:
                    pe.wait_ge(res_done, t)
                else:
                    pe.wait_ge(C_new, 32)
                for f in range(KC):
                    last = tr((B_, S_)[f // 4][0:n, P * (f % 4):P * (f % 4 + 1)], Y[:, f, t0:t0 + n])
                last.then_inc(mixT_ready, 1)

            def norm_T(t):
                t0, n = TILES[t]
                pe.wait_ge(ln_norm, t + 1)
                if t:
                    pe.wait_ge(xv_ready, KC * t)
                for f in range(KC):
                    last = tr((T_, D_)[f // 4][:, P * (f % 4):P * (f % 4) + n], RS[0:n, t % 2, P * f:P * (f + 1)])
                last.then_inc(nT_ready, 1)

            for u in range(U_OUT, U_FFN):
                b, j = (u - U_OUT) // 4, (u - U_OUT) % 4
                pe.wait_ge(lo_done, u + 1)

                def operands(k, b=b):
                    if k in (0, 4):
                        pe.wait_ge(cat_lo, 2 * b + (1 if k else 2))

                for f in range(2):
                    n = N_PROJ + 2 * (u - U_OUT) + f
                    if n < N_PROJ + 3:
                        pe.wait_ge(mixed_read, 10 + n - N_PROJ)
                    unit_product(u, f, b, n, (4, 5, 6, 7, 0, 1, 2, 3),
                                 operands if j == f == 0 else None).then_inc(gemm_done, 1)
                    if b == 0:
                        if u == U_OUT and f == 0:
                            for g in range(4):
                                last = tr(B_[0:NBUF + NS, P * g:P * (g + 1)], US[:, g, :])
                            last.then_inc(nat_T, 1)
                            pe.wait_ge(smp_n, 2)
                            pe.wait_ge(ncol_ready, NH)
                            tr(T_[0:32, 0:P], SM[:, 1, :, :].rearrange("p h b -> p (h b)"))
                            tr(T_[0:32, P:2 * P], ST[:, 8, :, :].rearrange("p h b -> p (h b)")).then_inc(kvs_T, 1)
                            tr(D_[0:36, 0:P], NO[:, :]).then_inc(nat_T, 1)
                        else:
                            pe.wait_ge(nat_read, 1)
                            outer(2 * j + f - 1)
                    else:
                        t = 3 * (b - 1) + j
                        if b == 1 and j == f == 0:
                            outer(7)
                        if f == 0 and j < 3:
                            mix_T(t)
                        elif f == 1 and j >= 1:
                            norm_T(t - 1)
            pe.sem_inc(down_done, 24)
            mix_T(6)

            def mlp_step(g, between=None, after=None):
                for i in range(12):
                    b, s, f = i // 4, U_FFN + i % 4 // 2, i % 2
                    n, cs = N_OUT + i, slice(P * f, P * (f + 1))
                    if i in (0, 2):
                        pe.wait_ge(lo_done, g * 4 + (s + 1))
                    if between and f == 0 and i % 4 == 0:
                        pe.wait_ge(x1_lo, 3 * (b + 1))
                    pe.wait_ge(gemm_read, g * 12 + (n - 2))
                    split_product(bank[n % 3][:, 0:BLK], lambda k: wslot(WH, s)[:, k, cs], lambda k: wslot(WL, s)[:, k, cs],
                                  lambda k: XH[:, k, blk(b)], lambda k: XL[:, k, blk(b)], range(KC)).then_inc(gemm_done, 1)
                    if between:
                        between(i)
                for m in range(24):
                    b, s, o = m // 8, U_FFN + 2 + m % 8 // 4, m % 4
                    cs = slice(P * o, P * (o + 1))
                    if m in (0, 4):
                        pe.wait_ge(lo_done, g * 4 + (s + 1))
                    if m % 8 == 0:
                        pe.wait_ge(h_lo, g * 12 + (2 + 4 * (b + 1)))
                    pe.wait_ge(down_read, g * 24 + (m + 1))
                    split_product(bank[3 + m % 3][:, 0:BLK], lambda k: wslot2(WH, s)[:, k, cs],
                                  lambda k: wslot2(WL, s)[:, k, cs], lambda k: HH[:, k, blk(b)],
                                  lambda k: HL[:, k, blk(b)], range(FG // P)).then_inc(down_done, 1)
                    if after:
                        after(m)

            def last_ln1(i):
                for kind, t in LN1_LAST.get(i, ()):
                    (mix_T, norm_T)[kind](t)

            def sum_T(t):
                t0, n = TILES[t]
                pe.wait_ge(down_read, 3 + 24 * (NG - 1) + KC * (t // 3 + 1))
                if 2 <= t < 8:
                    pe.wait_ge(l2_norm, 2 * (t - 1))
                for f in range(KC):
                    last = tr(bank[L2_BANK[t] + f // 4][0:n, P * (f % 4):P * (f % 4 + 1)], Y[:, f, t0:t0 + n])
                last.then_inc(l2_T, 1)

            def early_ln2(m):
                if m in LN2_EARLY:
                    sum_T(LN2_EARLY[m])

            mlp_step(0, last_ln1)
            with pe.Fori(1, NG - 1) as g:
                mlp_step(g)
            mlp_step(NG - 1, after=early_ln2)
            for t in (6, 7, 8):
                sum_T(t)


_OUTS = [("y_prompt", (1, 1024, 1024)), ("y_sample", (8, 1, 1024)), ("pool_p", (1, 1, 15, 512)),
         ("C_p", (1, 1, 4, 128, 128)), ("n_p", (1, 1, 4, 128)), ("m_p", (1, 1, 4)), ("pool_s", (1, 8, 15, 512)),
         ("C_s", (1, 8, 4, 128, 128)), ("n_s", (1, 8, 4, 128)), ("m_s", (1, 8, 4))]


def kernel(**inputs):
    import numpy as _np
    import concourse.bacc as _bacc
    from concourse import mybir as _mybir
    from concourse.bass_utils import run_bass_kernel_spmd as _run

    nc = _bacc.Bacc("TRN2", target_bir_lowering=False, num_devices=1)
    arrays, args = {}, {}
    for name, value in inputs.items():
        x = _np.ascontiguousarray(value)
        arrays[f"in_{name}"] = x
        args[name] = nc.dram_tensor(f"in_{name}", x.shape, _mybir.dt.from_np(x.dtype), kind="ExternalInput").ap()
    for name, shape in _OUTS:
        args[name] = nc.dram_tensor(f"out_{name}", shape, _mybir.dt.float32, kind="ExternalOutput").ap()
    build_layer(nc, args)
    r = _run(nc, [arrays], core_ids=[0])
    return tuple(r.results[0][f"out_{name}"] for name, _ in _OUTS)
```
